# Optimizing a Trainium2 kernel written in Bass

```python
import jax, jax.numpy as jnp
from jax import lax
import numpy as np

D_MODEL = 1024
BATCH = 1
SEQ = 1024
DEPTH = 2

N_MIXERS = 2
PLE_DIM = 256
CONV_DIM = D_MODEL
CONV_WIDTH = 31
HEAD_DIM = 64
HEADS_PER_GROUP = 8
DILATION_GROUPS = ((128, 1), (512, 4), (2048, 16))
N_GROUPS = len(DILATION_GROUPS)
QKV_DIM = N_GROUPS * HEADS_PER_GROUP * HEAD_DIM
ATTN_OUT_DIM = HEADS_PER_GROUP * HEAD_DIM
BLOCK = 128
ROPE_THETA = 500000.0
ROT_DIM = HEAD_DIM // 4
EPS = 1e-6
NEG_INF = -1e30
N_CONV_LAYERS = (DEPTH + 1) // 2
N_ATTN_LAYERS = DEPTH // 2
OUT_SCALE = (2.0 * DEPTH) ** -0.5
PLE_SCALE = 0.5


def rms_norm(x, g):
    x32 = x.astype(jnp.float32)
    y = x32 * lax.rsqrt(jnp.mean(x32 * x32, axis=-1, keepdims=True) + EPS)
    return (y * g.astype(jnp.float32)).astype(x.dtype)

def layer_norm(x, g, b):
    x32 = x.astype(jnp.float32)
    xc = x32 - jnp.mean(x32, axis=-1, keepdims=True)
    y = xc * lax.rsqrt(jnp.mean(xc * xc, axis=-1, keepdims=True) + EPS)
    return (y * g.astype(jnp.float32) + b.astype(jnp.float32)).astype(x.dtype)

def rope_tables(positions):
    inv_freq = 1.0 / (ROPE_THETA ** (jnp.arange(0, ROT_DIM, 2, dtype=jnp.float32) / ROT_DIM))
    ang = positions.astype(jnp.float32)[..., None] * inv_freq
    return jnp.cos(ang), jnp.sin(ang)

def partial_rope(x, cos, sin):
    c = cos[:, :, None, None, :]
    s = sin[:, :, None, None, :]
    half = ROT_DIM // 2
    xr = x[..., :ROT_DIM].astype(jnp.float32)
    x1, x2 = xr[..., :half], xr[..., half:]
    rot = jnp.concatenate([x1 * c - x2 * s, x2 * c + x1 * s], axis=-1).astype(x.dtype)
    return jnp.concatenate([rot, x[..., ROT_DIM:]], axis=-1)

def dilated_band_attention(q, k, v, dilation, band):
    B, S, H, hd = q.shape
    L = S // dilation
    nb = -(-L // BLOCK)
    Lp = nb * BLOCK

    def to_blocks(t):
        t = t.reshape(B, L, dilation, H, hd).transpose(0, 2, 1, 3, 4)
        t = jnp.pad(t, ((0, 0), (0, 0), (0, Lp - L), (0, 0), (0, 0)))
        return t.reshape(B, dilation, nb, BLOCK, H, hd)

    def with_prev(t):
        prev = jnp.pad(t, ((0, 0), (0, 0), (1, 0), (0, 0), (0, 0), (0, 0)))[:, :, :-1]
        return jnp.concatenate([prev, t], axis=3)

    qb, kb, vb = to_blocks(q), to_blocks(k), to_blocks(v)
    kk, vv = with_prev(kb), with_prev(vb)
    s = jnp.einsum('bdnqhc,bdnkhc->bdnhqk', qb, kk,
                   preferred_element_type=jnp.float32) * (hd ** -0.5)
    qi = jnp.arange(BLOCK)[:, None]
    kj = jnp.arange(2 * BLOCK)[None, :]
    dist = BLOCK + qi - kj
    blk = jnp.arange(nb)[:, None, None]
    valid = (dist >= 0) & (dist <= band) & (blk * BLOCK + kj - BLOCK >= 0)
    s = jnp.where(valid[:, None], s, NEG_INF)
    m = jnp.max(s, axis=-1, keepdims=True)
    e = jnp.exp(s - m)
    den = jnp.sum(e, axis=-1, keepdims=True)
    probs = (e / den).astype(v.dtype)
    o = jnp.einsum('bdnhqk,bdnkhc->bdnqhc', probs, vv)
    lse = (m + jnp.log(den))[..., 0]
    o = o.reshape(B, dilation, Lp, H, hd)[:, :, :L].transpose(0, 2, 1, 3, 4).reshape(B, S, H, hd)
    lse = lse.transpose(0, 1, 2, 4, 3).reshape(B, dilation, Lp, H)[:, :, :L]
    lse = lse.transpose(0, 2, 1, 3).reshape(B, S, H)
    return o, lse

def conformer_conv_branch(h, w_in, dw, dw_b, ln_g, ln_b, w_out):
    u = h @ w_in
    a, b, gate = jnp.split(u, [CONV_DIM, 2 * CONV_DIM], axis=-1)
    y = a * jax.nn.sigmoid(b)
    y = lax.conv_general_dilated(
        y, dw[:, None, :].astype(y.dtype), window_strides=(1,),
        padding=((CONV_WIDTH - 1, 0),), dimension_numbers=('NWC', 'WIO', 'NWC'),
        feature_group_count=CONV_DIM) + dw_b
    y = layer_norm(y, ln_g, ln_b)
    y = jax.nn.silu(y) * jax.nn.silu(gate)
    return y @ w_out

def dilated_attention_branch(h, cos, sin, w_in, q_norm, k_norm, w_out):
    B, S, _ = h.shape
    u = h @ w_in
    q, k, v, gate = jnp.split(u, [QKV_DIM, 2 * QKV_DIM, 3 * QKV_DIM], axis=-1)
    shp = (B, S, N_GROUPS, HEADS_PER_GROUP, HEAD_DIM)
    q = partial_rope(rms_norm(q.reshape(shp), q_norm), cos, sin)
    k = partial_rope(rms_norm(k.reshape(shp), k_norm), cos, sin)
    v = v.reshape(shp)
    outs, lses = [], []
    for g, (window, dilation) in enumerate(DILATION_GROUPS):
        o, lse = dilated_band_attention(q[:, :, g], k[:, :, g], v[:, :, g], dilation, window // dilation)
        outs.append(o)
        lses.append(lse)
    wts = jax.nn.softmax(jnp.stack(lses, axis=0), axis=0)
    o = jnp.sum(wts[..., None] * jnp.stack(outs, axis=0).astype(jnp.float32), axis=0).astype(h.dtype)
    y = o.reshape(B, S, ATTN_OUT_DIM) * jax.nn.silu(gate)
    return y @ w_out

def first_inputs(seed: int = 0) -> dict:
    key = jax.random.key(seed)
    ks = jax.random.split(key, 20)
    f32 = jnp.float32
    nrm = lambda k, shape: jax.random.normal(k, shape, dtype=f32)
    x = nrm(ks[0], (BATCH, SEQ, D_MODEL))
    p = nrm(ks[1], (DEPTH, BATCH, SEQ, PLE_DIM))
    offsets = jax.random.randint(ks[2], (BATCH, 1), 0, 1024, dtype=jnp.int32)
    positions = (jnp.arange(SEQ, dtype=jnp.int32)[None, :] + offsets).astype(jnp.int32)
    norm_g = 1.0 + 0.02 * nrm(ks[3], (DEPTH, D_MODEL))
    conv_w_in = nrm(ks[4], (N_CONV_LAYERS, D_MODEL, 3 * CONV_DIM)) * D_MODEL ** -0.5
    conv_dw = nrm(ks[5], (N_CONV_LAYERS, CONV_WIDTH, CONV_DIM)) * CONV_WIDTH ** -0.5
    conv_dw_b = 0.02 * nrm(ks[6], (N_CONV_LAYERS, CONV_DIM))
    conv_ln_g = 1.0 + 0.02 * nrm(ks[7], (N_CONV_LAYERS, CONV_DIM))
    conv_ln_b = 0.02 * nrm(ks[8], (N_CONV_LAYERS, CONV_DIM))
    conv_w_out = nrm(ks[9], (N_CONV_LAYERS, CONV_DIM, D_MODEL)) * (CONV_DIM ** -0.5 * OUT_SCALE)
    attn_w_in = nrm(ks[10], (N_ATTN_LAYERS, D_MODEL, 3 * QKV_DIM + ATTN_OUT_DIM)) * D_MODEL ** -0.5
    attn_q_norm = 1.0 + 0.02 * nrm(ks[11], (N_ATTN_LAYERS, HEAD_DIM))
    attn_k_norm = 1.0 + 0.02 * nrm(ks[12], (N_ATTN_LAYERS, HEAD_DIM))
    attn_w_out = nrm(ks[13], (N_ATTN_LAYERS, ATTN_OUT_DIM, D_MODEL)) * (ATTN_OUT_DIM ** -0.5 * OUT_SCALE)
    ple_w_proj = nrm(ks[14], (DEPTH, PLE_DIM, D_MODEL)) * (PLE_DIM ** -0.5 * PLE_SCALE)
    ple_norm_g = 1.0 + 0.02 * nrm(ks[15], (DEPTH, D_MODEL))
    ple_w_gate = nrm(ks[16], (DEPTH, D_MODEL, D_MODEL)) * D_MODEL ** -0.5
    return {'x': x, 'p': p, 'positions': positions, 'norm_g': norm_g,
            'conv_w_in': conv_w_in, 'conv_dw': conv_dw, 'conv_dw_b': conv_dw_b,
            'conv_ln_g': conv_ln_g, 'conv_ln_b': conv_ln_b, 'conv_w_out': conv_w_out,
            'attn_w_in': attn_w_in, 'attn_q_norm': attn_q_norm, 'attn_k_norm': attn_k_norm,
            'attn_w_out': attn_w_out, 'ple_w_proj': ple_w_proj, 'ple_norm_g': ple_norm_g,
            'ple_w_gate': ple_w_gate}

def first_block(x, p, positions, norm_g, conv_w_in, conv_dw, conv_dw_b, conv_ln_g, conv_ln_b,
              conv_w_out, attn_w_in, attn_q_norm, attn_k_norm, attn_w_out, ple_w_proj,
              ple_norm_g, ple_w_gate):
    cos, sin = rope_tables(positions)
    for i in range(DEPTH):
        h = rms_norm(x, norm_g[i])
        j = i // N_MIXERS
        if i % N_MIXERS == 0:
            x = x + conformer_conv_branch(h, conv_w_in[j], conv_dw[j], conv_dw_b[j],
                                          conv_ln_g[j], conv_ln_b[j], conv_w_out[j])
        else:
            x = x + dilated_attention_branch(h, cos, sin, attn_w_in[j], attn_q_norm[j],
                                             attn_k_norm[j], attn_w_out[j])
        gate = jax.nn.sigmoid(rms_norm(x, ple_norm_g[i]) @ ple_w_gate[i])
        x = x + (p[i] @ ple_w_proj[i]) * gate
    return x


DEPTH_2 = 1

GRID_W = 64
NA_HEADS = 8
NA_HEAD_DIM = 64
NA_WIDTH = NA_HEADS * NA_HEAD_DIM
NA_ROWS = 8
NA_COLS = 16
RET_HEADS = 4
RET_QK_DIM = 64
RET_V_DIM = 2 * RET_QK_DIM
RET_QK_WIDTH = RET_HEADS * RET_QK_DIM
RET_V_WIDTH = RET_HEADS * RET_V_DIM
RET_CHUNK = 128
ROPE_BASE = 10000.0
MIX_WIDTH = NA_WIDTH + RET_V_WIDTH
IN_WIDTH = 3 * NA_WIDTH + 2 * RET_QK_WIDTH + 2 * RET_V_WIDTH
D_FF = 4 * D_MODEL
NEG = -1e30


F32 = jnp.float32

def rms_norm_2(x, gain):
    x32 = x.astype(F32)
    y = x32 * lax.rsqrt(jnp.mean(jnp.square(x32), axis=-1, keepdims=True) + EPS)
    return (y * gain.astype(F32)).astype(x.dtype)

def head_group_norm(y, gain):
    bsz, seq, heads, dv = y.shape
    mu = jnp.mean(y, axis=-1, keepdims=True)
    var = jnp.mean(jnp.square(y - mu), axis=-1, keepdims=True)
    y = (y - mu) * lax.rsqrt(var + EPS)
    return y.reshape(bsz, seq, heads * dv) * gain.astype(F32)

def rotary(x, pos):
    d = x.shape[-1]
    inv = 1.0 / (ROPE_BASE ** (jnp.arange(0, d, 2, dtype=F32) / d))
    ang = pos.astype(F32)[:, None] * inv[None, :]
    cos = jnp.cos(ang)[None, :, None, :]
    sin = jnp.sin(ang)[None, :, None, :]
    x1, x2 = x[..., : d // 2], x[..., d // 2:]
    return jnp.concatenate([x1 * cos - x2 * sin, x1 * sin + x2 * cos], axis=-1)

def neighbourhood_attention(q, k, v, rpb):
    bsz, seq, heads, dh = q.shape
    rows = seq // GRID_W
    kh = min(NA_ROWS, rows)
    n_cb = GRID_W // NA_COLS
    band = 2 * NA_COLS
    col = np.arange(GRID_W)
    col_start = np.clip(col - NA_COLS // 2, 0, GRID_W - NA_COLS)
    band_start = np.clip(np.arange(n_cb) * NA_COLS - NA_COLS // 2, 0, GRID_W - band)
    band_idx = band_start[:, None] + np.arange(band)
    q_col = col.reshape(n_cb, NA_COLS)
    lo = col_start[q_col][..., None]
    kcol = band_idx[:, None, :]
    valid = jnp.asarray((kcol >= lo) & (kcol < lo + NA_COLS))
    dc = np.clip(kcol - q_col[..., None], -(NA_COLS - 1), NA_COLS - 1) + NA_COLS - 1
    bias_c = rpb.astype(F32)[:, :, dc]

    kb = k.reshape(bsz, rows, GRID_W, heads, dh)[:, :, band_idx]
    vb = v.reshape(bsz, rows, GRID_W, heads, dh)[:, :, band_idx]
    q_rows = jnp.moveaxis(q.reshape(bsz, rows, n_cb, NA_COLS, heads, dh), 1, 0)
    scale = dh ** -0.5

    def one_row(args):
        q_row, r = args
        rs = jnp.clip(r - kh // 2, 0, rows - kh)
        k_win = lax.dynamic_slice_in_dim(kb, rs, kh, axis=1)
        v_win = lax.dynamic_slice_in_dim(vb, rs, kh, axis=1)
        s = jnp.einsum('bcqhd,bicjhd->bhcqij', q_row, k_win).astype(F32) * scale
        dr = rs - r + jnp.arange(kh) + NA_ROWS - 1
        bias = jnp.take(bias_c, dr, axis=1)
        s = s + jnp.transpose(bias, (0, 2, 3, 1, 4))[None]
        s = jnp.where(valid[None, None, :, :, None, :], s, NEG)
        p = jax.nn.softmax(s.reshape(s.shape[:4] + (kh * band,)), axis=-1)
        p = p.reshape(s.shape).astype(v.dtype)
        return jnp.einsum('bhcqij,bicjhd->bcqhd', p, v_win)

    out = lax.map(one_row, (q_rows, jnp.arange(rows)))
    return jnp.moveaxis(out, 0, 1).reshape(bsz, seq, heads * dh)

def retention_scan(q, k, v, log_gamma, include_diag):
    bsz, seq, heads, dk = q.shape
    dv = v.shape[-1]
    c = RET_CHUNK
    n = seq // c
    qc = q.reshape(bsz, n, c, heads, dk)
    kc = k.reshape(bsz, n, c, heads, dk)
    vc = v.reshape(bsz, n, c, heads, dv)
    idx = jnp.arange(c, dtype=F32)
    diff = idx[:, None] - idx[None, :]
    keep = (diff >= 0) if include_diag else (diff > 0)
    dmat = jnp.where(keep[None], jnp.exp(log_gamma[:, None, None] * jnp.maximum(diff, 0.0)[None]), 0.0)
    s = jnp.einsum('bnihd,bnjhd->bnhij', qc, kc) * dmat
    intra = jnp.einsum('bnhij,bnjhe->bnihe', s, vc)
    zeta = jnp.exp(log_gamma[:, None] * (c - 1 - idx)[None, :])
    chunk_kv = jnp.einsum('bnjhd,hj,bnjhe->nbhde', kc, zeta, vc)
    chunk_decay = jnp.exp(log_gamma * c)[None, :, None, None]

    def step(state, kv):
        return chunk_decay * state + kv, state

    _, prev = lax.scan(step, jnp.zeros((bsz, heads, dk, dv), F32), chunk_kv)
    xi = jnp.exp(log_gamma[:, None] * (idx + 1.0)[None, :])
    cross = jnp.einsum('bnihd,nbhde,hi->bnihe', qc, prev, xi)
    return (intra + cross).reshape(bsz, seq, heads, dv)

def bidirectional_retention(q, k, v, lg_fwd, lg_bwd):
    flip = lambda t: jnp.flip(t, axis=1)
    fwd = retention_scan(q, k, v, lg_fwd, True)
    bwd = flip(retention_scan(flip(q), flip(k), flip(v), lg_bwd, False))
    return fwd + bwd

def log_decay(z):
    return jnp.log1p(-jnp.exp(z.astype(F32)))

def second_inputs(seed: int = 0) -> dict:
    key = jax.random.key(seed)
    ks = jax.random.split(key, 12)
    base_decay = -(5.0 + jnp.arange(RET_HEADS, dtype=F32)) * float(np.log(2.0))
    x = jax.random.normal(ks[0], (BATCH, SEQ, D_MODEL), F32)
    w_in = jax.random.normal(ks[1], (DEPTH_2, D_MODEL, IN_WIDTH), F32) * D_MODEL ** -0.5
    w_out = jax.random.normal(ks[2], (DEPTH_2, MIX_WIDTH, D_MODEL), F32) * MIX_WIDTH ** -0.5
    na_rpb = jax.random.normal(ks[3], (DEPTH_2, NA_HEADS, 2 * NA_ROWS - 1, 2 * NA_COLS - 1), F32) * 0.02
    ret_decay_fwd = base_decay[None] + 0.05 * jax.random.normal(ks[4], (DEPTH_2, RET_HEADS), F32)
    ret_decay_bwd = base_decay[None] + 0.05 * jax.random.normal(ks[5], (DEPTH_2, RET_HEADS), F32)
    ret_norm_gain = 1.0 + 0.02 * jax.random.normal(ks[6], (DEPTH_2, RET_V_WIDTH), F32)
    norm_mix = 1.0 + 0.02 * jax.random.normal(ks[7], (DEPTH_2, D_MODEL), F32)
    norm_mlp = 1.0 + 0.02 * jax.random.normal(ks[8], (DEPTH_2, D_MODEL), F32)
    w_up = jax.random.normal(ks[9], (DEPTH_2, D_MODEL, D_FF), F32) * D_MODEL ** -0.5
    w_down = jax.random.normal(ks[10], (DEPTH_2, D_FF, D_MODEL), F32) * D_FF ** -0.5
    norm_final = 1.0 + 0.02 * jax.random.normal(ks[11], (D_MODEL,), F32)
    return {'x': x, 'w_in': w_in, 'w_out': w_out, 'na_rpb': na_rpb,
            'ret_decay_fwd': ret_decay_fwd, 'ret_decay_bwd': ret_decay_bwd,
            'ret_norm_gain': ret_norm_gain, 'norm_mix': norm_mix, 'norm_mlp': norm_mlp,
            'w_up': w_up, 'w_down': w_down, 'norm_final': norm_final}

def second_block(x, w_in, w_out, na_rpb, ret_decay_fwd, ret_decay_bwd, ret_norm_gain,
              norm_mix, norm_mlp, w_up, w_down, norm_final):
    bsz, seq, _ = x.shape
    pos = jnp.arange(seq)
    splits = np.cumsum([NA_WIDTH, NA_WIDTH, NA_WIDTH, RET_QK_WIDTH, RET_QK_WIDTH, RET_V_WIDTH])
    for l in range(DEPTH_2):
        h = rms_norm_2(x, norm_mix[l])
        proj = h @ w_in[l]
        na_q, na_k, na_v, r_q, r_k, r_v, r_g = jnp.split(proj, splits, axis=-1)
        na_out = neighbourhood_attention(na_q.reshape(bsz, seq, NA_HEADS, NA_HEAD_DIM),
                                         na_k.reshape(bsz, seq, NA_HEADS, NA_HEAD_DIM),
                                         na_v.reshape(bsz, seq, NA_HEADS, NA_HEAD_DIM),
                                         na_rpb[l])
        rq = rotary(r_q.reshape(bsz, seq, RET_HEADS, RET_QK_DIM).astype(F32), pos)
        rk = rotary(r_k.reshape(bsz, seq, RET_HEADS, RET_QK_DIM).astype(F32), pos) * RET_QK_DIM ** -0.5
        rv = r_v.reshape(bsz, seq, RET_HEADS, RET_V_DIM).astype(F32)
        ret = bidirectional_retention(rq, rk, rv, log_decay(ret_decay_fwd[l]), log_decay(ret_decay_bwd[l]))
        ret = head_group_norm(ret, ret_norm_gain[l])
        ret_out = (jax.nn.silu(r_g.astype(F32)) * ret).astype(x.dtype)
        mix = jnp.concatenate([na_out.astype(x.dtype), ret_out], axis=-1)
        x = x + mix @ w_out[l]
        h = rms_norm_2(x, norm_mlp[l])
        x = x + jnp.square(jax.nn.relu(h @ w_up[l])) @ w_down[l]
    return rms_norm_2(x, norm_final)


def setup_inputs(seed=0):
    out = dict(first_inputs(seed))
    for name, value in second_inputs(seed + 1).items():
        if name != "x":
            out[name + "_2"] = value
    return out


def reference(
    x, p, positions, norm_g, conv_w_in, conv_dw, conv_dw_b, conv_ln_g, conv_ln_b, conv_w_out,
    attn_w_in, attn_q_norm, attn_k_norm, attn_w_out, ple_w_proj, ple_norm_g, ple_w_gate, w_in_2,
    w_out_2, na_rpb_2, ret_decay_fwd_2, ret_decay_bwd_2, ret_norm_gain_2, norm_mix_2,
    norm_mlp_2, w_up_2, w_down_2, norm_final_2,
):
    x = first_block(
        x, p, positions, norm_g, conv_w_in, conv_dw, conv_dw_b, conv_ln_g, conv_ln_b,
        conv_w_out, attn_w_in, attn_q_norm, attn_k_norm, attn_w_out, ple_w_proj, ple_norm_g,
        ple_w_gate,
    )
    return second_block(
        x, w_in_2, w_out_2, na_rpb_2, ret_decay_fwd_2, ret_decay_bwd_2, ret_norm_gain_2,
        norm_mix_2, norm_mlp_2, w_up_2, w_down_2, norm_final_2,
    )


_drawn_inputs = setup_inputs


def setup_inputs(seed=0):
    import zlib

    import numpy as np

    out = dict(_drawn_inputs(seed))
    spreads = {}
    factors = {'norm_g': 8.0,
     'conv_dw_b': 6.37,
     'conv_ln_g': 8.0,
     'conv_ln_b': 8.0,
     'attn_q_norm': 8.0,
     'attn_k_norm': 8.0,
     'ple_norm_g': 64.0,
     'na_rpb_2': 200.0,
     'ret_norm_gain_2': 51.17,
     'norm_mix_2': 10.303,
     'norm_mlp_2': 51.744,
     'norm_final_2': 19.182}
    for name, (base, spread) in spreads.items():
        noise = np.random.default_rng([zlib.crc32(name.encode()), seed]).standard_normal(out[name].shape)
        drawn = base * np.exp(spread * noise) if base else spread * noise
        out[name] = __import__('jax').numpy.asarray(drawn.astype(out[name].dtype))
    for name, factor in factors.items():
        out[name] = (out[name] * factor).astype(out[name].dtype)
    return out
```

```python
from collections import defaultdict
from contextlib import ExitStack, contextmanager

import concourse.bass as bass
from concourse import mybir

F32 = mybir.dt.float32
F32R = mybir.dt.float32r
I32 = mybir.dt.int32
ALU = mybir.AluOpType
ACT = mybir.ActivationFunctionType
AX = mybir.AxisListType

P = 128
D = 1024
T = 1024
KT = D // P
HALF = 512
PLE_K = 2
CONV_W = 31
PAD = CONV_W - 1
HD = 64
PAIRS = 4
GROUPS = 3
BLOCKS = T // P
GRID_W = 64
NA_ROWS = 8
RET_HEADS = 4
FF_CHUNKS = 4
EPS = 1e-6
NEG = -1e30
SCALE = HD**-0.5
ROUND = 12582912.0
PI = 3.1415925
INV_TWO_PI = 0.15915494309189535
RPB_COLS = 2 * 16 - 1
RPB_ROW = RPB_COLS * GRID_W
RPB_HEAD = (2 * NA_ROWS - 1) * RPB_ROW
TWO_PI_PARTS = (6.28125, 0.0019350051879882812, 3.0199157663446e-07)

POOL_TAPS = 11

W_TILES = {"conv_in": 24, "conv_out": 8, "ple0": 8, "attn": PAIRS * 10, "attn_out": 4, "ple1": 8,
           "na": PAIRS * 3, "ret": 12, "mix_out": 8, "mlp": 64}
N_W = sum(W_TILES.values())

VEC = {}
_at = 0
for _name, _n in (("norm0", 8), ("ple0", 8), ("norm1", 8), ("ple1", 8), ("mix", 8), ("mlp", 8), ("final", 8),
                  ("dw_b", 8), ("ln_g", 8), ("ln_b", 8), ("ret_gain", 4), ("q_gain", 1), ("k_gain", 1),
                  ("inv_freq", 1)):
    VEC[_name] = _at
    _at += _n
N_VEC = _at

NA_KEYS = [(0, 4, False), (0, 4, False), (0, 5, True), (1, 5, True), (2, 5, True), (3, 5, True),
           (4, 4, False), (4, 4, False)]
NA_ALL = 14
NA_INNER = 10


RAISED = {"ab_free0": "pe", "ab_free1": "pe", "w_ready0": "sp", "w_ready1": "sp", "r_out": "act", "u_ready": "act"}


class Tally:

    def __init__(self):
        self.base = defaultdict(int, {name: 1 for name in RAISED})
        self.loops = []
        self.cd = 0
        self.ab = 0

    def now(self, name, back=0):
        at = self.base[name] - back
        for i, per in self.loops:
            at = i * per.get(name, 0) + at
        return at

    def next(self, name, n=1):
        self.base[name] += n
        return self.now(name)

    @contextmanager
    def loop(self, eng, count, **per):
        start = dict(self.base)
        with eng.Fori(0, count) as i:
            self.loops.append((i, per))
            yield i
            self.loops.pop()
        found = {k: v - start.get(k, 0) for k, v in self.base.items() if v != start.get(k, 0)}
        assert found == per, f"one pass raises {found}"
        for k, v in per.items():
            self.base[k] = start.get(k, 0) + count * v


class Region:

    def __init__(self, nc, *spans):
        self.nc, self.spans = nc, [list(s) for s in spans]

    def take(self, name, shape, dt=F32):
        n = 4
        for x in shape[1:]:
            n *= x
        for span in self.spans:
            if span[1] - span[0] >= n:
                at = span[0]
                span[0] += -(-n // 32) * 32
                self.at = at
                return self.nc.alloc_sbuf_tensor_at(name, shape, dt, offset=at)
        raise ValueError(f"no room for {name}")


def build(nc, x, p, positions, vecs, dw, w, wp, rpb, decay, masks, na_masks, rot, mats, diffs, stats_dram, out):
    with ExitStack() as ctx:
        SEMS = {}

        class Semaphores(dict):
            def __missing__(self, name):
                self[name] = ctx.enter_context(nc.semaphore(name))
                return self[name]

        S = Semaphores()

        base = -(-nc.sbuf_base // 64) * 64
        end = nc.sbuf_usable_end
        KB = 1024
        X0, HA0, HB0, W0, M0 = base, base + 32 * KB, base + 96 * KB, base + 160 * KB, base + 184 * KB
        all_x = Region(nc, (X0, HA0))
        X = all_x.take("X", [P, KT, T])

        def split_pair(name, at, tiles):
            r = Region(nc, (at, at + 2 * tiles * 4 * KB))
            return r.take(name + "_hi", [P, tiles, T], F32R), r.take(name + "_lo", [P, tiles, T], F32R)

        HA = split_pair("HA", HA0, KT)
        HB = split_pair("HB", HB0, KT)
        rw = Region(nc, (W0, M0))
        w_raw = [rw.take(f"w_raw{i}", [P, KT, P]) for i in range(2)]
        w_hi = [rw.take(f"w_hi{i}", [P, KT, P], F32R) for i in range(2)]
        w_lo = [rw.take(f"w_lo{i}", [P, KT, P], F32R) for i in range(2)]
        rm = Region(nc, (M0, end))
        rstd = rm.take("rstd", [P, T])
        vec = rm.take("vec", [P, N_VEC])
        ones = rm.take("ones", [P, P])
        ident = rm.take("ident", [P, P])
        head_ones = rm.take("head_ones", [P, P])
        perm = rm.take("perm", [P, P])
        eps = rm.take("eps", [P, 1])
        free0 = rm.spans[0][0]
        rt = Region(nc, (free0, end))
        ssum = rt.take("ssum", [P, T])
        sq = rt.take("sq", [P, T])
        ta = rt.take("ta", [P, T])
        wp_sb = [rt.take(f"wp_sb{i}", [P, PLE_K, P]) for i in range(2)]

        def col(name, k=0, n=1):
            return vec[:, VEC[name] + k:VEC[name] + k + n]

        def dcol(name, k):
            return vec[:, bass.ds(k + VEC[name], 1)]

        rc = Region(nc, (X0, HA0))
        ypad = [rc.take(f"ypad{i}", [P, PAD + T]) for i in range(2)]
        sig = rc.take("sig", [P, T])
        acc1 = rc.take("acc1", [P, T])
        accp = rc.take("accp", [P, T])
        dw_sb = rc.take("dw_sb", [P, KT, CONV_W])
        act_dw = rc.take("act_dw", [P, CONV_W])
        tap_out = [rc.take(f"tap_out{i}", [P, T]) for i in range(2)]

        def dw_col(c, j):
            return dw_sb[:, bass.ds(c, 1), j:j + 1].rearrange("p a b -> p (a b)")

        ry = Region(nc, (HB0, W0))
        Y = ry.take("Y", [P, KT, T])
        G = ry.take("G", [P, KT, T])

        def side(tag, at):
            a = Region(nc, (at + 28 * KB, at + 32 * KB)).take(f"p_{tag}0", [P, T])
            b = Region(nc, (at + 60 * KB, at + 64 * KB)).take(f"p_{tag}1", [P, T])
            return a, b

        ra = Region(nc, (HB0, W0), (free0, end))
        y_at = ra.take("y_at", [P, PAIRS, T])
        qT, kT, vT, q_in, k_in, cosT, sinT = (
            ra.take(n, [P, T]) for n in ("qT", "kT", "vT", "q_in", "k_in", "cosT", "sinT"))
        V = ra.take("V", [P, BLOCKS, P])
        O = ra.take("O", [P, GROUPS, BLOCKS, P])
        tmp = ra.take("tmp", [P, T])
        mask = ra.take("mask", [P, 3 * P])
        st = ra.take("st", [P, GROUPS, BLOCKS, 2, 2])
        st_x = ra.take("st_x", [P, GROUPS, GROUPS, BLOCKS, 2, 2])
        cw = ra.take("cw", [P, 3, GROUPS * GROUPS * BLOCKS * 2])
        q_root = ra.take("q_root", [P, T])
        at_q = Region(nc, (ra.at, ra.at + 4 * KB))
        sc = [at_q.take(f"sc{i}", [P, 2, 2 * P]) for i in range(2)]
        k_root = ra.take("k_root", [P, T])
        at_k = Region(nc, (ra.at, ra.at + 4 * KB))
        pt = [at_k.take(f"pt{i}", [P, 4 * P]) for i in range(2)]
        m1 = vT
        pos_i = Region(nc, (HB0 + 16 * KB, W0)).take("pos_i", [P, T], I32)
        YS = split_pair("YS", HB0 + 32 * KB, PAIRS)

        rmix = Region(nc, (HA0, HB0), (free0, end))
        mix = rmix.take("mix", [P, KT, T])
        nqT, nkT, nvT = (rmix.take(n, [P, T]) for n in ("nqT", "nkT", "nvT"))
        nV = rmix.take("nV", [P, BLOCKS, P])
        na_mask = rmix.take("na_mask", [P, NA_ALL + NA_INNER, GRID_W])
        bias = [rmix.take(f"bias{h}", [P, NA_ALL + NA_INNER, GRID_W]) for h in range(2)]
        nO = rmix.take("nO", [P, BLOCKS, 2, HD])
        NK = 5 * P
        nsc = [rmix.take(f"nsc{i}", [P, NK]) for i in range(2)]
        npt = [rmix.take(f"npt{i}", [P, NK]) for i in range(2)]
        nst = rmix.take("nst", [P, 2, 2, BLOCKS])
        rr = Region(nc, (HA0 + 32 * KB, HB0), (free0, end))
        rqT, rkT, rtmp, rcos, rsin = (rr.take(n, [P, T]) for n in ("rqT", "rkT", "rtmp", "rcos", "rsin"))
        rV = rr.take("rV", [P, BLOCKS, P])
        SPAN = T + (BLOCKS - 1) * P
        decay_t = rr.take("decay_t", [P, SPAN])
        sd = rr.take("sd", [P, 2, T])
        d_neg = Region(nc, (rr.at, rr.at + 8 * KB)).take("d_neg", [P, SPAN])
        lg = rr.take("lg", [P, 2, RET_HEADS])
        r_root, r_m1 = (rr.take(n, [P, T]) for n in ("r_root", "r_m1"))

        def lg_col(way, head):
            return lg[:, way, bass.ds(head, 1)]

        p_a, p_b = side("A", HA0), side("B", HB0)

        AB = [ctx.enter_context(nc.psum_tensor(f"ps_{n}", [P, T], F32)) for n in "AB"]
        CD = [ctx.enter_context(nc.psum_tensor(f"ps_{n}", [P, T], F32)) for n in "CD"]
        OC = T - HD

        block = ctx.enter_context(nc.Block())

        UNITS = [(h, b) for h in range(2) for b in range(BLOCKS)]

        def attn_keys(g, b):
            own = (b, 1, P if g < 2 else 2 * P)
            if (g == 0 and b > 0) or (g == 1 and b % 2):
                return b - 1, 2, 0
            return own

        RES = (1, 4, 16)

        def by_residue(g, t):
            return t[:, :] if g == 0 else t[:, :].rearrange("p (t r) -> p r t", r=RES[g])

        def grouped(g, t):
            return t[:, :] if g == 0 else t[:, :].rearrange("p (r t) -> p r t", r=RES[g])

        def stats_moves(tile, own, g):
            tile = tile.rearrange("p b h s -> p b (h s)")
            d = stats_dram[g]
            if own == 0:
                return [(tile, d.rearrange("(b p) s -> p b s", p=P))]
            if own == 1:
                return [(tile[:, c::2, :], d[c * HALF:(c + 1) * HALF].rearrange("(p r) s -> p r s", r=4))
                        for c in range(2)]
            d = d.rearrange("(i b r) s -> r i b s", b=BLOCKS, r=2)
            return [(tile[c * HD:(c + 1) * HD], d[c]) for c in range(2)]

        @block.sync
        def _(sp):
            n = Tally()
            def weight_pair(t):
                for q in range(2):
                    sp.wait_ge(S[f"w_ready{q}"], n.now(f"w_ready{q}"))
                    n.next(f"w_ready{q}")
                    sp.dma_start(w_raw[q][:, :, :], w[t + q]).then_inc(S[f"w_loaded{q}"], 16)

            for q in range(2):
                sp.sem_inc(S[f"w_ready{q}"], 1)
            sp.dma_start(vec[:, :], vecs).then_inc(S["vec_loaded"], 16)
            sp.dma_start(ones[:, :], mats[0]).then_inc(S["ones_loaded"], 16)
            for k in range(KT):
                if k == 1:
                    weight_pair(0)
                sp.dma_start(X[:, k, :], x[k]).then_inc(S[f"x_loaded{k}"], 16)
            sp.dma_start(ident[:, :], mats[1]).then_inc(S["ident_loaded"], 16)
            sp.dma_start(head_ones[:, :], mats[2]).then_inc(S["head_ones_loaded"], 16)
            sp.dma_start(perm[:, :], mats[3]).then_inc(S["perm_loaded"], 16)

            with n.loop(sp, N_W // 2 - 1, w_ready0=1, w_ready1=1) as i:
                weight_pair(i * 2 + 2)
            for k in range(KT):
                sp.wait_ge(S["out_ready"], k + 1)
                sp.dma_start(out[k], X[:, k, :]).then_inc(S["stored"], 16)
            sp.wait_ge(S["stored"], 16 * KT)

        @block.gpsimd
        def _(pool):
            n = Tally()

            def settle():
                pool.sem_inc(S["pool_settled"], 1)

            def split_lo(q):
                pool.wait_ge(S["w_rounded"], n.next("w_rounded"))
                pool.tensor_tensor(w_lo[q][:, :, :], w_raw[q][:, :, :], w_hi[q][:, :, :].bitcast(F32),
                                   ALU.subtract).then_inc(S[f"w_ready{q}"], 1)

            def split_weights(q):
                pool.wait_ge(S[f"w_loaded{q}"], n.next(f"w_loaded{q}", 16))
                pool.wait_ge(S[f"lin_done{q}"], n.next(f"lin_done{q}"))
                settle()
                pool.tensor_copy(w_hi[q][:, :, :], w_raw[q][:, :, :]).then_inc(S["w_rounded"], 1)
                split_lo(q)

            ADDS = POOL_TAPS - 1
            ADD_ENDS = (0, ADDS // 3, 2 * ADDS // 3, ADDS)

            def add_taps(part):
                for j in range(ADD_ENDS[part], ADD_ENDS[part + 1]):
                    if j == 0:
                        pool.wait_ge(S["tap_product"], n.next("tap_product"))
                        pool.wait_ge(S["y_ready"], n.now("y_ready"))
                        n.next("y_ready")
                    pool.wait_ge(S["tap_product"], n.next("tap_product"))
                    if j > 0:
                        pool.wait_ge(S["pool_tap"], n.now("pool_tap"))
                    pool.tensor_tensor(accp[:, :], (tap_out[0] if j == 0 else accp)[:, :],
                                       tap_out[(j + 1) % 2][:, :], ALU.add).then_inc(S["pool_tap"], 1)
                    n.next("pool_tap")

            def conv_pass(first):
                for u in range(2):
                    for part in range(3):
                        split_lo((3 * u + part) % 2)
                        if not (first and u == 0):
                            add_taps(part)

            split_lo(0)
            split_lo(1)
            conv_pass(True)
            with n.loop(pool, KT // 2 - 1, w_rounded=6, tap_product=2 * POOL_TAPS, y_ready=2, pool_tap=2 * ADDS):
                conv_pass(False)
            for part in range(3):
                add_taps(part)
            for q in range(2):
                n.next(f"w_loaded{q}", 16 * (W_TILES["conv_in"] // 2 + 1))
                n.next(f"lin_done{q}", W_TILES["conv_in"] // 2)
            with n.loop(pool, (N_W - W_TILES["conv_in"]) // 2 - 1, w_loaded0=16, w_loaded1=16, lin_done0=1,
                        lin_done1=1, w_rounded=2):
                split_weights(0)
                split_weights(1)

        @block.tensor
        def _(pe):
            n = Tally()

            def take_ab():
                b = n.ab
                n.ab ^= 1
                pe.wait_ge(S[f"ab_free{b}"], n.now(f"ab_free{b}"))
                n.next(f"ab_free{b}")
                return b

            def take_cd():
                b = n.cd
                n.cd ^= 1
                pe.wait_ge(S[f"cd_free{b}"], n.now(f"cd_free{b}"))
                n.next(f"cd_free{b}")
                return b

            def products(b, q, h, ks, w0=0, first=True, last=True):
                hi, lo = h
                for k in ks:
                    for step, (wt, act) in enumerate(((w_hi[q], hi), (w_hi[q], lo), (w_lo[q], hi))):
                        for c in range(2):
                            cols = slice(c * HALF, (c + 1) * HALF)
                            op = pe.matmul(AB[b][:, cols], wt[:, w0 + k, :], act[:, k, cols],
                                           start=(first and k == ks[0] and step == 0),
                                           stop=(last and k == ks[-1] and step == 2))
                return op

            def linear(q, h, pre=None):
                pe.wait_ge(S[f"w_ready{q}"], n.next(f"w_ready{q}"))
                b = take_ab()
                for k in range(KT):
                    if pre:
                        pre(k)
                    op = products(b, q, h, [k], first=(k == 0), last=(k == KT - 1))
                op.then_inc(S[f"lin_done{q}"], 1)
                return b

            def column_sums(src, m, b, first=True, last=True):
                for c in range(2):
                    cols = slice(c * HALF, (c + 1) * HALF)
                    op = pe.matmul(CD[b][:, cols], m[:, :], src[:, cols], start=first, stop=last)
                return op

            def norm_stats():
                pe.wait_ge(S["ssum_added"], n.next("ssum_added", KT))
                column_sums(ssum, ones, take_cd()).then_inc(S["stats_done"], 1)

            def opening(q, h):
                split = n.base["h_ready"]
                linear(q, h, pre=lambda k: pe.wait_ge(S["h_ready"], split + k + 1))
                n.next("h_ready", KT)
                norm_stats()

            for b in range(2):
                pe.sem_inc(S[f"ab_free{b}"], 1)
            pe.wait_ge(S["ones_loaded"], 16)
            opening(0, HA)
            for t in range(1, 6):
                linear(t % 2, HA)
            with n.loop(pe, KT // 2 - 1, w_ready0=3, w_ready1=3, ab_free0=3, ab_free1=3):
                for t in range(6):
                    linear(t % 2, HA)
            b = take_cd()
            for k in range(KT):
                pe.wait_ge(S["y_ready"], k + 1)
                op = column_sums(Y[:, k, :], ones, b, k == 0, k == KT - 1)
            op.then_inc(S["y_sum_done"], 1)
            b = take_cd()
            for k in range(KT):
                pe.wait_ge(S["y_sq_ready"], k + 1)
                column_sums((sq, ta)[k % 2], ones, b, k == 0, k == KT - 1).then_inc(S["y_sq_used"], 1)

            def z_ready(k):
                pe.wait_ge(S["z_ready"], k + 1)

            linear(0, HA, pre=z_ready)
            linear(1, HA)
            with n.loop(pe, KT // 2 - 1, w_ready0=1, w_ready1=1, ab_free0=1, ab_free1=1):
                for t in range(2):
                    linear(t, HA)

            def gated_side(h, p_sb):
                def side_tile(t):
                    pe.wait_ge(S[f"wp_loaded{t}"], n.next(f"wp_loaded{t}", 16))
                    b = take_ab()
                    for k in range(PLE_K):
                        for c in range(2):
                            cols = slice(c * HALF, (c + 1) * HALF)
                            op = pe.matmul(AB[b][:, cols], wp_sb[t][:, k, :], p_sb[k][:, cols],
                                           start=(k == 0), stop=(k == PLE_K - 1))
                    op.then_inc(S["side_done"], 1)

                opening(0, h)
                for q in range(2):
                    pe.wait_ge(S[f"p_loaded{q}"], n.next(f"p_loaded{q}", 16))
                side_tile(0)
                linear(1, h)
                side_tile(1)
                with n.loop(pe, KT // 2 - 1, w_ready0=1, w_ready1=1, ab_free0=2, ab_free1=2, wp_loaded0=16,
                            wp_loaded1=16):
                    for t in range(2):
                        linear(t, h)
                        side_tile(t)

            gated_side(HB, p_a)

            def scores(u, keys, q, k):
                h, bq = UNITS[u]
                k0, nk = keys(bq)
                b = take_ab()
                rows = slice(HD * h, HD * h + HD)
                for c in range(0, nk, 4):
                    cn = min(4, nk - c)
                    op = pe.matmul(AB[b][:, c * P:(c + cn) * P], q[rows, bq * P:(bq + 1) * P],
                                   k[rows, (k0 + c) * P:(k0 + c + cn) * P], start=True, stop=True)
                op.then_inc(S["scores_done"], 1)

            def turn(src, count):
                b = take_cd()
                for c in range(count):
                    op = pe.transpose(CD[b][:, c * P:(c + 1) * P], src(c), ident[:, :])
                return b, op

            def values(u, b, keys, t, v):
                h, bq = UNITS[u]
                k0, nk = keys(bq)
                pe.wait_ge(S["turned_copied"], n.next("turned_copied"))
                for c in range(nk):
                    op = pe.matmul(CD[b][:, OC:T], t[u % 2][:, c * P:(c + 1) * P],
                                   v[:, k0 + c, HD * h:HD * h + HD], start=(c == 0), stop=(c == nk - 1))
                op.then_inc(S["unit_done"], 1)

            def attention(keys, q, k, v_t, s, t, v):
                slots = {}
                for u in range(len(UNITS) + 2):
                    if u < len(UNITS):
                        scores(u, keys, q, k)
                    if u == 1:
                        turn(lambda c: v_t[:, c * P:(c + 1) * P], BLOCKS)[1].then_inc(S["v_turned"], 1)
                    if 1 <= u <= len(UNITS):
                        pe.wait_ge(S["probs_ready"], n.next("probs_ready"))
                        _, nk = keys(UNITS[u - 1][1])
                        slots[u - 1], op = turn(lambda c: s[(u - 1) % 2][:, c * P:(c + 1) * P], nk)
                        op.then_inc(S["turned"], 1)
                    if u >= 2:
                        values(u - 2, slots[u - 2], keys, t, v)

            def dilated(g):
                slots = {}
                for u in range(BLOCKS + 2):
                    if u < BLOCKS:
                        k0, nk, _ = attn_keys(g, u)
                        b = take_ab()
                        for h in range(2):
                            rows = slice(HD * h, HD * h + HD)
                            op = pe.matmul(AB[b][:, h * HALF:h * HALF + nk * P], qT[rows, u * P:(u + 1) * P],
                                           kT[rows, k0 * P:(k0 + nk) * P], start=True, stop=True)
                        op.then_inc(S["scores_done"], 1)
                    if u == 1:
                        turn(lambda c: vT[:, c * P:(c + 1) * P], BLOCKS)[1].then_inc(S["v_turned"], 1)
                    if 1 <= u <= BLOCKS:
                        pe.wait_ge(S["probs_ready"], n.next("probs_ready"))
                        nk, s = attn_keys(g, u - 1)[1], sc[(u - 1) % 2]
                        slots[u - 1], op = turn(lambda c: s[:, c // nk, c % nk * P:(c % nk + 1) * P], 2 * nk)
                        op.then_inc(S["turned"], 1)
                    if u >= 2:
                        k0, nk, _ = attn_keys(g, u - 2)
                        pe.wait_ge(S["turned_copied"], n.next("turned_copied"))
                        for h in range(2):
                            for c in range(nk):
                                at = (h * nk + c) * P
                                op = pe.matmul(CD[slots[u - 2]][:, T - P + HD * h:T - P + HD * h + HD],
                                               pt[u % 2][:, at:at + P], V[:, k0 + c, HD * h:HD * h + HD],
                                               start=(c == 0), stop=(c == nk - 1))
                        op.then_inc(S["unit_done"], 1)

            def rope_parts(src, name):
                pe.wait_ge(S[name + "_sq"], n.next(name + "_sq"))
                column_sums(tmp, head_ones, take_cd()).then_inc(S[name + "_sum"], 1)
                pe.wait_ge(S[name + "_gained"], n.next(name + "_gained"))
                column_sums(src, perm, take_cd()).then_inc(S[name + "_swapped"], 1)

            def qkv(q, g, first=False):
                if first:
                    opening(q, HA)
                else:
                    linear(q, HA)
                linear(q ^ 1, HA)
                rope_parts(q_in, "q")
                pe.wait_ge(S[f"w_ready{q}"], n.next(f"w_ready{q}"))
                b = take_ab()
                products(b, q, HA, range(KT // 2), last=False)
                rope_parts(k_in, "k")
                products(b, q, HA, range(KT // 2, KT), first=False).then_inc(S[f"lin_done{q}"], 1)

            def combine():
                pe.wait_ge(S["O_scaled"], n.next("O_scaled"))
                b = take_cd()
                for c in range(2):
                    half = CD[b][:, c * HALF:(c + 1) * HALF]
                    todo = [(0, 4 * c + i, half[:, i * P:(i + 1) * P], ident[:, :]) for i in range(4)]
                    todo += [(1, 2 * r + c, half.rearrange("p (t r) -> p r t", r=4)[:, r, :], ident[:, :])
                             for r in range(4)]
                    todo += [(2, r // 2, half.rearrange("p (t r) -> p r t", r=16)[:, r, :],
                              ident[:, (r % 2) * HD + c * 32:(r % 2) * HD + c * 32 + 32]) for r in range(16)]
                    for i, (g, blk, dst, sel) in enumerate(todo):
                        op = pe.matmul(dst, O[:, g, blk, :], sel, start=(i == 0), stop=(i == len(todo) - 1),
                                       skip_group_check=True)
                op.then_inc(S["combined"], 1)

            def pair(last):
                for g in range(GROUPS):
                    if g > 0:
                        qkv(g % 2, g)
                    pe.wait_ge(S["qk_ready"], n.next("qk_ready"))
                    dilated(g)
                linear(1, HA)
                if not last:
                    qkv(0, 0)
                combine()

            for name in ("head_ones_loaded", "perm_loaded", "ident_loaded"):
                pe.wait_ge(S[name], 16)
            qkv(0, 0, first=True)
            with n.loop(pe, PAIRS - 1, w_ready0=5, w_ready1=5, ab_free0=17, ab_free1=17, cd_free0=20, cd_free1=20,
                        q_sq=3, q_gained=3, k_sq=3, k_gained=3, qk_ready=3, probs_ready=24, turned_copied=24,
                        O_scaled=1):
                pair(last=False)
            pair(last=True)

            def ys_ready(k):
                pe.wait_ge(S["ys_ready"], k + 1)

            def out_half(t, half, pre=None):
                if half == 0:
                    pe.wait_ge(S[f"w_ready{t}"], n.next(f"w_ready{t}"))
                b = take_ab()
                for k in range(PAIRS):
                    if pre:
                        pre(k)
                    op = products(b, t, YS, [k], w0=half * PAIRS, first=(k == 0), last=(k == PAIRS - 1))
                op.then_inc(S["half_done"] if half == 0 else S[f"lin_done{t}"], 1)

            out_half(0, 0, ys_ready)
            out_half(0, 1)
            out_half(1, 0)
            out_half(1, 1)
            for t in range(2):
                out_half(t, 0)
                out_half(t, 1)
            gated_side(HA, p_b)

            norm_stats()
            pe.wait_ge(S["h_ready"], n.next("h_ready", KT))
            with n.loop(pe, PAIRS // 2, w_ready0=3, w_ready1=3, ab_free0=19, ab_free1=19, cd_free0=18, cd_free1=18,
                        probs_ready=32, turned_copied=32, nO_scaled=2):
                def turn_out():
                    pe.wait_ge(S["nO_scaled"], n.next("nO_scaled"))
                    turn(lambda c: nO[:, c, :, :].rearrange("p h d -> p (h d)"), BLOCKS)[1] \
                        .then_inc(S["combined"], 1)

                for t in range(2):
                    linear(t, HB)
                    linear(t ^ 1, HB)
                    if t == 1:
                        turn_out()
                    linear(t, HB)
                    attention(lambda bq: NA_KEYS[bq][:2], nqT, nkT, nvT, nsc, npt, nV)
                turn_out()

            pe.wait_ge(S["rperm_loaded"], 16)
            with n.loop(pe, RET_HEADS // 2, w_ready0=3, w_ready1=3, ab_free0=11, ab_free1=11, cd_free0=5, cd_free1=5,
                        rqk_ready=1, r_sq_ready=2):
                def evacuated(b):
                    pe.wait_ge(S[f"ab_free{b}"], n.now(f"ab_free{b}"))

                bq = linear(0, HB)
                bk = linear(1, HB)
                evacuated(bq)
                column_sums(rqT, perm, take_cd()).then_inc(S["rq_swapped"], 1)
                evacuated(bk)
                column_sums(rkT, perm, take_cd()).then_inc(S["rk_swapped"], 1)
                for h in range(2):
                    rows = slice(HD * h, HD * h + HD)
                    bv = linear(0, HB)
                    linear(1, HB)
                    evacuated(bv)
                    turn(lambda c: rtmp[:, c * P:(c + 1) * P], BLOCKS)[1].then_inc(S["v_turned"], 1)
                    if h == 0:
                        pe.wait_ge(S["rqk_ready"], n.next("rqk_ready"))
                    slots = []
                    for jt in range(BLOCKS + 1):
                        if jt < BLOCKS:
                            b = take_ab()
                            slots.append(b)
                            for c in range(2):
                                cols = slice(c * HALF, (c + 1) * HALF)
                                op = pe.matmul(AB[b][:, cols], rkT[rows, jt * P:(jt + 1) * P], rqT[rows, cols],
                                               start=True, stop=True)
                            op.then_inc(S["rs_done"], 1)
                        if jt == 1:
                            turned = n.cd ^ 1
                            pe.wait_ge(S[f"cd_free{turned}"], n.now(f"cd_free{turned}"))
                            out_b = take_cd()
                        if jt >= 1:
                            evacuated(slots[jt - 1])
                            for c in range(2):
                                cols = slice(c * HALF, (c + 1) * HALF)
                                op = pe.matmul(CD[out_b][:, cols], rV[:, jt - 1, :], sd[:, (jt - 1) % 2, cols],
                                               start=(jt == 1), stop=(jt == BLOCKS))
                            op.then_inc(S["sd_used"], 1)
                    pe.wait_ge(S[f"cd_free{out_b}"], n.now(f"cd_free{out_b}"))
                    column_sums(rtmp, ones, take_cd()).then_inc(S["r_sum"], 1)
                    pe.wait_ge(S["r_sq_ready"], n.next("r_sq_ready"))
                    column_sums(sd[:, 0, :], ones, take_cd()).then_inc(S["r_var"], 1)

            def mix_ready(k):
                pe.wait_ge(S["mix_ready"], k + 1)

            linear(0, HB, pre=mix_ready)
            linear(1, HB)
            with n.loop(pe, KT // 2 - 1, w_ready0=1, w_ready1=1, ab_free0=1, ab_free1=1):
                for t in range(2):
                    linear(t, HB)

            def down():
                def u_ready(k):
                    pe.wait_ge(S["u_ready"], n.next("u_ready"))

                linear(0, HB, pre=u_ready)
                for t in range(1, KT):
                    linear(t % 2, HB)

            opening(0, HA)
            for t in range(1, KT):
                linear(t % 2, HA)
            down()
            with n.loop(pe, FF_CHUNKS - 1, w_ready0=8, w_ready1=8, ab_free0=8, ab_free1=8, u_ready=KT):
                for t in range(KT):
                    linear(t % 2, HA)
                down()
            norm_stats()

        @block.scalar
        def _(act):
            n = Tally()

            def settle():
                if n.loops:
                    act.sem_inc(S["act_settled"], 1)

            def after(name):
                act.wait_ge(S[name], n.next(name))

            def pass_ab(count=1):
                for _ in range(count):
                    n.next(f"ab_free{n.ab}")
                    n.ab ^= 1

            def after_ab():
                b = n.ab
                n.ab ^= 1
                act.wait_ge(S[f"ab_free{b}"], n.next(f"ab_free{b}"))

            def next_cd():
                b = n.cd
                n.cd ^= 1
                n.next(f"cd_free{b}")
                return b, S[f"cd_free{b}"]

            def inverse_root(dst, b, scale, done):
                act.activation(dst, CD[b][:, :], ACT.Ln, scale=scale, bias=eps[:, :]).then_inc(S[f"cd_free{b}"], 1)
                act.wait_ge(S[f"cd_free{b}"], n.now(f"cd_free{b}"))
                act.activation(dst, dst, ACT.Exp, scale=-0.5).then_inc(S[done], 1)

            def norm_stats():
                after("stats_done")
                b, _ = next_cd()
                inverse_root(rstd[:, :], b, 1.0 / D, "rstd_ready")

            def absorb(gain, hi, xs):
                settle()
                act.activation(hi, xs, ACT.Identity, scale=gain).then_inc(S["hi_ready"], 1)
                act.wait_ge(S["ssum_added"], n.now("ssum_added"))
                n.next("ssum_added")
                settle()
                act.activation(sq[:, :], xs, ACT.Square).then_inc(S["sq_ready"], 1)

            def round_weights(q, first=False):
                act.wait_ge(S[f"w_loaded{q}"], n.next(f"w_loaded{q}", 16))
                if not first:
                    act.wait_ge(S[f"lin_done{q}"], n.next(f"lin_done{q}"))
                act.copy(w_hi[q][:, :, :], w_raw[q][:, :, :]).then_inc(S["w_rounded"], 1)

            for name in ("r_out", "u_ready"):
                act.sem_inc(S[name], 1)
            act.wait_ge(S["vec_loaded"], 16)
            act.wait_ge(S["consts_set"], 1)
            for k in range(KT):
                act.wait_ge(S[f"x_loaded{k}"], 16)
                absorb(col("norm0", k), HA[0][:, k, :], X[:, k, :])
                if k in (1, 3):
                    round_weights(k // 2, first=True)
            act.wait_ge(S["ssum_added"], KT)
            act.dma_start(dw_sb[:, :, :], dw).then_inc(S["dw_loaded"], 16)
            norm_stats()

            TAP_ENDS = (0, POOL_TAPS // 3, 2 * POOL_TAPS // 3, POOL_TAPS)

            def tap_products(u, c, part):
                if part == 0:
                    act.wait_ge(S["glu_ready"], n.next("glu_ready"))
                    act.wait_ge(S["tap_product"], n.now("tap_product"))
                    settle()
                    act.copy(act_dw[:, :], dw_sb[:, bass.ds(c, 1), :].rearrange("p a b -> p (a b)")) \
                        .then_inc(S["act_dw_ready"], 1)
                    act.wait_ge(S["act_dw_ready"], n.next("act_dw_ready"))
                for j in range(TAP_ENDS[part], TAP_ENDS[part + 1]):
                    at = CONV_W - POOL_TAPS + j
                    if j != 1:
                        sums = 0 if j == 0 else max(j - 2, 1)
                        act.wait_ge(S["pool_tap"], n.now("pool_tap") + sums)
                    act.activation(tap_out[j % 2][:, :], ypad[u][:, at:at + T], ACT.Identity,
                                   scale=act_dw[:, at:at + 1]).then_inc(S["tap_product"], 1)
                    n.next("tap_product")
                if part == 2:
                    n.next("pool_tap", POOL_TAPS - 1)

            def conv_pass(channel, first):
                for u in range(2):
                    c = channel + u
                    go = not (first and u == 0)
                    pass_ab()
                    round_weights(u)
                    if go:
                        tap_products(u ^ 1, c - 1, 0)
                    round_weights(u ^ 1)
                    after_ab()
                    act.activation(sig[:, :], sig[:, :], ACT.Sigmoid).then_inc(S["sig_ready"], 1)
                    if go:
                        tap_products(u ^ 1, c - 1, 1)
                    round_weights(u)
                    after_ab()
                    settle()
                    act.activation(G[:, c, :], G[:, c, :], ACT.Silu).then_inc(S["gate_silu"], 1)
                    if go:
                        tap_products(u ^ 1, c - 1, 2)

            act.wait_ge(S["dw_loaded"], 16)
            conv_pass(0, True)
            with n.loop(act, KT // 2 - 1, ab_free0=3, ab_free1=3, w_loaded0=48, w_loaded1=48, lin_done0=3,
                        lin_done1=3, glu_ready=2, act_dw_ready=2, pool_tap=2 * (POOL_TAPS - 1),
                        tap_product=2 * POOL_TAPS) as i:
                conv_pass(i * 2 + 2, False)
            for part in range(3):
                tap_products((KT - 1) % 2, KT - 1, part)
            act.wait_ge(S["y_ready"], KT)
            for k in range(KT):
                act.dma_start(X[:, k, :], x[k]).then_inc(S[f"x_loaded{k}"], 16)
            after("y_sum_done")
            b, free = next_cd()
            act.activation(ssum[:, :], CD[b][:, :], ACT.Identity, scale=1.0 / D).then_inc(free, 1)
            for k in range(KT):
                after("y_centred")
                if k >= 2:
                    act.wait_ge(S["y_sq_used"], k - 1)
                act.activation((sq, ta)[k % 2][:, :], Y[:, k, :], ACT.Square).then_inc(S["y_sq_ready"], 1)
            act.wait_ge(S["y_sq_used"], KT)
            b, _ = next_cd()
            inverse_root(ssum[:, :], b, 1.0 / D, "ln_rstd_ready")
            for k in range(KT + 1):
                if k < KT:
                    after("ln_scaled")
                    act.activation(Y[:, k, :], Y[:, k, :], ACT.Silu, scale=col("ln_g", k),
                                   bias=col("ln_b", k)).then_inc(S["ln_silu"], 1)
                if k >= 1:
                    after("ln_gated")
                    act.copy(HA[0][:, k - 1, :], Y[:, k - 1, :]).then_inc(S["z_hi"], 1)

            def absorb_sum(name, h):
                with n.loop(act, KT // 2, ab_free0=1, ab_free1=1, ssum_added=2) as i:
                    for t in range(2):
                        after_ab()
                        absorb(dcol(name, i * 2 + t), h[0][:, i * 2 + t, :], X[:, i * 2 + t, :])

            absorb_sum("ple0", HB)

            def gated_side(layer, name, h, p_sb):
                for q in range(2):
                    act.dma_start(p_sb[q][:, :], p[layer, q]).then_inc(S[f"p_loaded{q}"], 16)
                for q in range(2):
                    act.dma_start(wp_sb[q][:, :, :], wp[layer, q]).then_inc(S[f"wp_loaded{q}"], 16)
                norm_stats()

                def side_pass(i, last):
                    for t in range(2):
                        m = i * 2 + t
                        after_ab()
                        act.activation(ta[:, :], ta[:, :], ACT.Sigmoid).then_inc(S["side_gate"], 1)
                        pass_ab()
                        after("x_new")
                        absorb(dcol(name, m), h[0][:, m, :], X[:, m, :])
                        if not last:
                            act.dma_start(wp_sb[t][:, :, :], wp[layer, m + 2]).then_inc(S[f"wp_loaded{t}"], 16)

                with n.loop(act, KT // 2 - 1, ab_free0=2, ab_free1=2, x_new=2, ssum_added=2) as i:
                    side_pass(i, False)
                side_pass(KT // 2 - 1, True)

            gated_side(0, "norm1", HA, p_a)

            norm_stats()
            act.dma_start(pos_i[:, :], bass.AP(tensor=positions.tensor, offset=0, ap=[[0, P], [1, T]])) \
                .then_inc(S["pos_loaded"], 16)
            act.dma_start(mask[:, :], masks).then_inc(S["mask_loaded"], 16)

            def attention(keys, s, t, v, stats):
                def probabilities(u):
                    h, bq = UNITS[u]
                    nk = keys(bq)[1]
                    after_ab()
                    act.activation(s[u % 2][:, 0:nk * P], s[u % 2][:, 0:nk * P], ACT.Exp, scale=-1.0,
                                   bias=stats(h, bq, 0), accum_out=stats(h, bq, 1)).then_inc(S["probs_ready"], 1)

                probabilities(0)
                probabilities(1)
                after("v_turned")
                b, free = next_cd()
                act.copy(v[:, :, :].rearrange("p b d -> p (b d)"), CD[b][:, :]).then_inc(free, 1)
                for u in range(len(UNITS)):
                    nk = keys(UNITS[u][1])[1]
                    after("turned")
                    b, _ = next_cd()
                    if u >= 2:
                        after("unit_done")
                    act.copy(t[u % 2][:, 0:nk * P], CD[b][:, 0:nk * P]).then_inc(S["turned_copied"], 1)
                    if u + 2 < len(UNITS):
                        probabilities(u + 2)
                after("unit_done")
                after("unit_done")

            def dilated(g):
                def probabilities(u):
                    nk = attn_keys(g, u)[1]
                    after_ab()
                    for h in range(2):
                        s = sc[u % 2][:, h, 0:nk * P]
                        op = act.activation(s, s, ACT.Exp, scale=-1.0, bias=st[:, g, u, h, 0:1],
                                            accum_out=st[:, g, u, h, 1:2])
                    op.then_inc(S["probs_ready"], 1)

                probabilities(0)
                probabilities(1)
                after("v_turned")
                b, free = next_cd()
                act.copy(V[:, :, :].rearrange("p b d -> p (b d)"), CD[b][:, :]).then_inc(free, 1)
                for u in range(BLOCKS):
                    nk = attn_keys(g, u)[1]
                    after("turned")
                    b, _ = next_cd()
                    if u >= 2:
                        after("unit_done")
                    act.copy(pt[u % 2][:, 0:2 * nk * P], CD[b][:, 0:2 * nk * P]).then_inc(S["turned_copied"], 1)
                    if u + 2 < BLOCKS:
                        probabilities(u + 2)
                after("unit_done")
                after("unit_done")

            def roots():
                for name, src, root in (("q", q_in, q_root), ("k", k_in, k_root)):
                    after_ab()
                    act.activation(tmp[:, :], src[:, :], ACT.Square).then_inc(S[name + "_sq"], 1)
                    act.activation(src[:, :], src[:, :], ACT.Identity, scale=col(name + "_gain")) \
                        .then_inc(S[name + "_gained"], 1)
                    after(name + "_sum")
                    b, _ = next_cd()
                    inverse_root(root[:, :], b, 1.0 / HD, name + "_root_ready")
                    next_cd()
                pass_ab()

            def pair(j, last):
                for g in range(GROUPS):
                    if g > 0:
                        roots()
                    dilated(g)
                    act.wait_ge(S["probs_ready"], n.next("probs_ready", BLOCKS))
                    for src, dst in stats_moves(st[:, g], g, g):
                        act.dma_start(dst, src).then_inc(S["stats_stored"], 16)
                        n.next("stats_stored", 16)
                act.wait_ge(S["stats_stored"], n.now("stats_stored"))
                for own in range(GROUPS):
                    for g in range(GROUPS):
                        for dst, src in stats_moves(st_x[:, own, g], own, g):
                            act.dma_start(dst, src).then_inc(S["stats_seen"], 16)
                            n.next("stats_seen", 16)
                after_ab()
                settle()
                act.activation(y_at[:, j, :], y_at[:, j, :], ACT.Silu).then_inc(S["gate_silu"], 1)
                after("shift_ready")
                act.activation(cw[:, 0, :], cw[:, 0, :], ACT.Exp).then_inc(S["share_ready"], 1)
                if not last:
                    roots()
                next_cd()

            roots()
            after("angle_ready")
            act.activation(cosT[:, :], qT[:, :], ACT.Sin, scale=0.5).then_inc(S["half_sin"], 1)
            act.activation(sinT[:, :], qT[:, :], ACT.Sin).then_inc(S["sin_ready"], 1)
            with n.loop(act, PAIRS - 1, ab_free0=17, ab_free1=17, cd_free0=20, cd_free1=20, q_sum=3, k_sum=3,
                        v_turned=3, turned=24, unit_done=24, probs_ready=24, stats_stored=80, stats_seen=240,
                        shift_ready=1) as j:
                pair(j, last=False)
            pair(PAIRS - 1, last=True)
            b = n.cd ^ 1
            act.wait_ge(S[f"cd_free{b}"], n.now(f"cd_free{b}"))
            for k in range(PAIRS):
                act.copy(YS[0][:, k, :], y_at[:, k, :]).then_inc(S["ys_hi"], 1)
            absorb_sum("ple1", HA)
            gated_side(1, "mix", HB, p_b)

            norm_stats()
            act.dma_start(na_mask[:, :, :], na_masks).then_inc(S["na_mask_loaded"], 16)

            def load_bias(pair):
                for h in range(2):
                    for d0, count, at in ((1, NA_ALL, 0), (3, NA_INNER, NA_ALL)):
                        for par in (1, 0):
                            row = (pair * 2 + h) * RPB_HEAD + ((d0 - par) * RPB_ROW + RPB_COLS // 2)
                            src = bass.AP(tensor=rpb.tensor, offset=row,
                                          ap=[[RPB_COLS - 1, GRID_W], [RPB_ROW, count], [1, GRID_W]])
                            act.dma_start(bias[h][par * GRID_W:(par + 1) * GRID_W, at:at + count, :], src) \
                                .then_inc(S["bias_loaded"], 16)

            n.next("combined", PAIRS)
            with n.loop(act, PAIRS // 2, ab_free0=19, ab_free1=19, cd_free0=18, cd_free1=18, v_turned=2,
                        turned=32, unit_done=32, combined=2) as i:
                for t in range(2):
                    pair = i * 2 + t
                    if t == 0:
                        load_bias(pair)
                    pass_ab(3)
                    attention(lambda bq: NA_KEYS[bq][:2], nsc, npt, nV,
                              lambda h, bq, w: nst[:, h, w, bq:bq + 1])
                    if t == 0:
                        load_bias(pair + 1)
                    after("combined")
                    b, free = next_cd()
                    settle()
                    act.copy(mix[:, pair, :], CD[b][:, :]).then_inc(free, 1)

            act.wait_ge(free, n.now(f"cd_free{b}"))
            act.dma_start(perm[:, :], mats[4]).then_inc(S["rperm_loaded"], 16)
            act.dma_start(rcos[:, :], rot[0]).then_inc(S["rcos_loaded"], 16)
            act.dma_start(rsin[:, :], rot[1]).then_inc(S["rsin_loaded"], 16)
            act.dma_start(lg[:, :, :], decay).then_inc(S["decay_loaded"], 16)
            act.wait_ge(S["decay_loaded"], 16)
            act.activation(lg[:, :, :], lg[:, :, :], ACT.Exp).then_inc(S["gamma_ready"], 1)
            act.wait_ge(S["gamma_ready"], 1)
            act.activation(lg[:, :, :], lg[:, :, :], ACT.Ln, scale=-1.0, bias=1.0).then_inc(S["gamma_ready"], 1)
            act.wait_ge(S["gamma_ready"], 2)
            with n.loop(act, RET_HEADS // 2, ab_free0=11, ab_free1=11, cd_free0=5, cd_free1=5, v_turned=2,
                        decay_arg=2, r_var=2, sd_used=16) as i:
                pass_ab(2)
                next_cd()
                next_cd()
                for h in range(2):
                    act.wait_ge(S["r_out"], n.now("decay_arg") + 1)
                    act.dma_start(decay_t[:, :], diffs).then_inc(S["diffs_loaded"], 16)
                    pass_ab()
                    after_ab()
                    gate = mix[:, i * 2 + h + PAIRS, :]
                    settle()
                    act.activation(gate, gate, ACT.Silu).then_inc(S["gate_silu"], 1)
                    after("decay_arg")
                    act.activation(decay_t[:, :], decay_t[:, :], ACT.Exp).then_inc(S["decay_ready"], 1)
                    after("v_turned")
                    b, free = next_cd()
                    act.copy(rV[:, :, :].rearrange("p b d -> p (b d)"), CD[b][:, :]).then_inc(free, 1)
                    pass_ab(BLOCKS)
                    act.wait_ge(S["sd_used"], n.next("sd_used", BLOCKS))
                    b, free = next_cd()
                    act.activation(rtmp[:, :], CD[b][:, :], ACT.Identity, scale=SCALE).then_inc(free, 1)
                    b, free = next_cd()
                    act.wait_ge(free, n.now(f"cd_free{b}"))
                    act.activation(sd[:, 0, :], rtmp[:, :], ACT.Square).then_inc(S["r_sq_ready"], 1)
                    after("r_var")
                    b, _ = next_cd()
                    inverse_root(r_root[:, :], b, 1.0 / P, "r_root_ready")
            for k in range(KT):
                act.wait_ge(S["r_out"], RET_HEADS + 1)
                act.copy(HB[0][:, k, :], mix[:, k, :]).then_inc(S["mix_hi"], 1)
            absorb_sum("mlp", HA)

            norm_stats()
            with n.loop(act, FF_CHUNKS, ab_free0=8, ab_free1=8, u_sq=KT, u_ready=KT):
                for t in range(KT):
                    after_ab()
                    act.wait_ge(S["u_ready"], n.now("u_ready"))
                    n.next("u_ready")
                    act.activation(sq[:, :], ta[:, :], ACT.Square).then_inc(S["u_sq"], 1)
                    act.wait_ge(S["u_sq"], n.next("u_sq"))
                    act.copy(HB[0][:, t, :], sq[:, :]).then_inc(S["u_hi"], 1)
                pass_ab(KT)
            for b in range(2):
                act.wait_ge(S[f"ab_free{b}"], n.now(f"ab_free{b}"))
            for k in range(KT):
                act.wait_ge(S["ssum_added"], n.now("ssum_added", 0))
                n.next("ssum_added")
                act.activation(sq[:, :], X[:, k, :], ACT.Square).then_inc(S["sq_ready"], 1)
            norm_stats()

        @block.vector
        def _(dve):
            n = Tally()

            def after(name, count=1):
                dve.wait_ge(S[name], n.next(name, count))

            def next_ab():
                b = n.ab
                n.ab ^= 1
                n.next(f"ab_free{b}")
                return b, S[f"ab_free{b}"]

            def next_cd():
                b = n.cd
                n.cd ^= 1
                n.next(f"cd_free{b}")
                return b, S[f"cd_free{b}"]

            def settle():
                if n.loops:
                    dve.sem_inc(S["dve_settled"], 1)

            def step(op):
                op.then_inc(S["dve_step"], 1)
                dve.wait_ge(S["dve_step"], n.next("dve_step"))

            def absorb(gain, h, k, xs):
                after("hi_ready")
                dve.scalar_tensor_tensor(h[1][:, k, :], xs, gain, h[0][:, k, :].bitcast(F32), ALU.mult,
                                         ALU.subtract).then_inc(S["h_ready"], 1)
                after("sq_ready")
                dve.wait_ge(S["ssum_added"], n.now("ssum_added"))
                dve.tensor_tensor(ssum[:, :], ssum[:, :], sq[:, :], ALU.add).then_inc(S["ssum_added"], 1)
                n.next("ssum_added")

            def clear_sum():
                if n.base["ssum_added"]:
                    after("stats_done")
                step(dve.memset(ssum[:, :], 0.0))

            dve.memset(eps[:, :], EPS).then_inc(S["consts_set"], 1)
            dve.wait_ge(S["vec_loaded"], 16)
            clear_sum()
            for k in range(KT):
                dve.wait_ge(S[f"x_loaded{k}"], 16)
                absorb(col("norm0", k), HA, k, X[:, k, :])
            dve.wait_ge(S["h_ready"], KT)
            for u in range(2):
                step(dve.memset(ypad[u][:, 0:PAD], 0.0))
            dve.wait_ge(S["dw_loaded"], 16)
            next_cd()
            after("rstd_ready")

            def evacuate(dst, q, ps=None):
                after(f"lin_done{q}")
                b, free = next_ab()
                dve.tensor_tensor(dst, AB[b][:, :] if ps is None else ps(AB[b]),
                                  rstd[:, :] if ps is None else ps(rstd), ALU.mult).then_inc(free, 1)
                return b

            TAPS = CONV_W - POOL_TAPS
            ENDS = (0, TAPS // 3, 2 * TAPS // 3, TAPS)

            def taps(u, c, part):
                for j in range(ENDS[part], ENDS[part + 1]):
                    tap, win = dw_col(c, j), ypad[u][:, j:j + T]
                    acc = (Y[:, c, :], acc1[:, :])[j % 2]
                    dve.wait_ge(S["dve_tap"], n.now("dve_tap", 1))
                    if j == 0:
                        op = dve.tensor_scalar(acc, win, tap, dcol("dw_b", c), ALU.mult, ALU.add)
                    elif j == 1:
                        op = dve.tensor_scalar(acc, win, tap, None, ALU.mult)
                    else:
                        op = dve.scalar_tensor_tensor(acc, win, tap, acc, ALU.mult, ALU.add)
                    op.then_inc(S["dve_tap"], 1)
                    n.next("dve_tap")
                if part == 2:
                    dve.wait_ge(S["dve_tap"], n.now("dve_tap"))
                    dve.tensor_tensor(Y[:, c, :], Y[:, c, :], acc1[:, :], ALU.add).then_inc(S["dve_tap"], 1)
                    dve.wait_ge(S["dve_tap"], n.next("dve_tap"))
                    after("pool_tap", POOL_TAPS - 1)
                    dve.tensor_tensor(Y[:, c, :], Y[:, c, :], accp[:, :], ALU.add).then_inc(S["y_ready"], 1)
                    dve.wait_ge(S["y_ready"], n.next("y_ready"))

            def conv_pass(channel, first):
                for u in range(2):
                    c, prev = channel + u, channel + u - 1
                    go = not (first and u == 0)
                    q = u
                    b = evacuate(ypad[u][:, PAD:], q)
                    dve.wait_ge(S[f"ab_free{b}"], n.now(f"ab_free{b}"))
                    if go:
                        taps(u ^ 1, prev, 0)
                    evacuate(sig[:, :], q ^ 1)
                    if go:
                        taps(u ^ 1, prev, 1)
                    evacuate(G[:, c, :], q)
                    if go:
                        taps(u ^ 1, prev, 2)
                    after("sig_ready")
                    dve.tensor_tensor(ypad[u][:, PAD:], ypad[u][:, PAD:], sig[:, :], ALU.mult) \
                        .then_inc(S["glu_ready"], 1)
                    dve.wait_ge(S["glu_ready"], n.next("glu_ready"))

            step_once = dve.memset(acc1[:, 0:1], 0.0)
            step_once.then_inc(S["dve_tap"], 1)
            n.next("dve_tap")
            conv_pass(0, True)
            with n.loop(dve, KT // 2 - 1, ab_free0=3, ab_free1=3, lin_done0=3, lin_done1=3, sig_ready=2, glu_ready=2,
                        dve_tap=2 * (TAPS + 1), pool_tap=2 * (POOL_TAPS - 1), y_ready=2) as i:
                conv_pass(i * 2 + 2, False)
            for part in range(3):
                taps((KT - 1) % 2, KT - 1, part)
            b, free = next_cd()
            dve.wait_ge(free, n.now(f"cd_free{b}"))
            for k in range(KT):
                dve.tensor_tensor(Y[:, k, :], Y[:, k, :], ssum[:, :], ALU.subtract).then_inc(S["y_centred"], 1)
            next_cd()
            after("ln_rstd_ready")
            dve.wait_ge(S["gate_silu"], n.next("gate_silu", KT))
            for k in range(KT + 2):
                if k < KT:
                    dve.tensor_tensor(Y[:, k, :], Y[:, k, :], ssum[:, :], ALU.mult).then_inc(S["ln_scaled"], 1)
                if 1 <= k <= KT:
                    after("ln_silu")
                    dve.tensor_tensor(Y[:, k - 1, :], Y[:, k - 1, :], G[:, k - 1, :], ALU.mult) \
                        .then_inc(S["ln_gated"], 1)
                if k >= 2:
                    after("z_hi")
                    dve.tensor_tensor(HA[1][:, k - 2, :], Y[:, k - 2, :], HA[0][:, k - 2, :].bitcast(F32),
                                      ALU.subtract).then_inc(S["z_ready"], 1)
            for k in range(KT):
                dve.wait_ge(S[f"x_loaded{k}"], 32)

            def absorb_sum(name, h, halves=False):
                clear_sum()
                per = dict(half_done=1, lin_done0=1) if halves else dict(lin_done0=1, lin_done1=1)

                def one(m, done):
                    after(done)
                    b, free = next_ab()
                    dve.tensor_tensor(X[:, m, :], X[:, m, :], AB[b][:, :], ALU.add).then_inc(free, 1)
                    dve.wait_ge(free, n.now(f"ab_free{b}"))
                    absorb(dcol(name, m), h, m, X[:, m, :])

                if halves:
                    for m in range(KT):
                        one(m, "half_done" if m % 2 == 0 else f"lin_done{(m // 2) % 2}")
                else:
                    with n.loop(dve, KT // 2, ab_free0=1, ab_free1=1, hi_ready=2, sq_ready=2, ssum_added=2,
                                **per) as i:
                        for t in range(2):
                            one(i * 2 + t, f"lin_done{t}")

            absorb_sum("ple0", HB)

            def gated_side(name, h):
                clear_sum()
                next_cd()
                after("rstd_ready")
                with n.loop(dve, KT // 2, ab_free0=2, ab_free1=2, hi_ready=2, sq_ready=2, ssum_added=2, lin_done0=1,
                            lin_done1=1, side_gate=2, side_done=2, x_new=2) as i:
                    for t in range(2):
                        m = i * 2 + t
                        evacuate(ta[:, :], t)
                        after("side_gate")
                        after("side_done")
                        b, free = next_ab()
                        dve.tensor_tensor(ta[:, :], AB[b][:, :], ta[:, :], ALU.mult).then_inc(free, 1)
                        dve.wait_ge(free, n.now(f"ab_free{b}"))
                        dve.tensor_tensor(X[:, m, :], X[:, m, :], ta[:, :], ALU.add).then_inc(S["x_new"], 1)
                        dve.wait_ge(S["x_new"], n.next("x_new"))
                        absorb(dcol(name, m), h, m, X[:, m, :])

            gated_side("norm1", HA)

            next_cd()
            after("rstd_ready")
            def attention(keys, s, bias_of, out_of, stats):
                def softmax_input(u):
                    h, bq = UNITS[u]
                    nk = keys(bq)[1]
                    after("scores_done")
                    if u >= 2:
                        after("turned")
                    b, free = next_ab()
                    settle()
                    dve.tensor_tensor_reduce(s[u % 2][:, 0:nk * P], AB[b][:, 0:nk * P], bias_of(h, bq), -SCALE,
                                             3e38, ALU.add, ALU.min, stats(h, bq, 0)).then_inc(free, 1)

                softmax_input(0)
                softmax_input(1)
                next_cd()
                for u in range(len(UNITS)):
                    if u + 2 < len(UNITS):
                        softmax_input(u + 2)
                    after("unit_done")
                    b, free = next_cd()
                    dve.tensor_copy(out_of(*UNITS[u]), CD[b][:, OC:T]).then_inc(free, 1)
                after("turned", 2)

            def dilated(g):
                def softmax_input(u):
                    _, nk, m = attn_keys(g, u)
                    after("scores_done")
                    if u >= 2:
                        after("turned")
                    b, free = next_ab()
                    settle()
                    for h in range(2):
                        op = dve.tensor_tensor_reduce(sc[u % 2][:, h, 0:nk * P],
                                                      AB[b][:, h * HALF:h * HALF + nk * P], mask[:, m:m + nk * P],
                                                      -SCALE, 3e38, ALU.add, ALU.min, st[:, g, u, h, 0:1])
                    op.then_inc(free, 1)

                softmax_input(0)
                softmax_input(1)
                next_cd()
                for u in range(BLOCKS):
                    if u + 2 < BLOCKS:
                        softmax_input(u + 2)
                    after("unit_done")
                    b, free = next_cd()
                    dve.tensor_copy(O[:, g, u, :], CD[b][:, T - P:T]).then_inc(free, 1)
                after("turned", 2)

            def rope(name, src, root, dst, g):
                after(name + "_swapped")
                step(dve.tensor_tensor(src[:, :], src[:, :], cosT[:, :], ALU.mult))
                b, free = next_cd()
                dve.tensor_tensor(m1[:, :], CD[b][:, :], sinT[:, :], ALU.mult).then_inc(free, 1)
                dve.wait_ge(free, n.now(f"cd_free{b}"))
                step(dve.tensor_tensor(src[:, :], src[:, :], m1[:, :], ALU.add))
                after(name + "_root_ready")
                return dve.tensor_tensor(grouped(g, dst), by_residue(g, src), by_residue(g, root), ALU.mult)

            def rotary_tables():
                dve.wait_ge(S["pos_loaded"], 16)
                step(dve.tensor_copy(kT[:, :], pos_i[:, :]))
                step(dve.tensor_scalar(qT[:, :], kT[:, :], col("inv_freq"), None, ALU.mult))
                step(dve.tensor_scalar(kT[:, :], qT[:, :], INV_TWO_PI, ROUND, ALU.mult, ALU.add))
                step(dve.tensor_scalar(kT[:, :], kT[:, :], ROUND, None, ALU.subtract))
                for part in TWO_PI_PARTS:
                    step(dve.scalar_tensor_tensor(qT[:, :], kT[:, :], -part, qT[:, :], ALU.mult, ALU.add))
                dve.tensor_scalar(qT[:, :], qT[:, :], PI, -PI, ALU.min, ALU.max).then_inc(S["angle_ready"], 1)
                after("half_sin")
                step(dve.tensor_tensor(cosT[:, :], cosT[:, :], cosT[:, :], ALU.mult))
                step(dve.tensor_scalar(cosT[:, :], cosT[:, :], -2.0, 1.0, ALU.mult, ALU.add))
                after("sin_ready")
                dve.wait_ge(S["mask_loaded"], 16)

            def qkv(q, g, between=None):
                evacuate(q_in[:, :], q)
                evacuate(k_in[:, :], q ^ 1)
                if between:
                    between()
                next_cd()
                step(rope("q", q_in, q_root, qT, g))
                next_cd()
                rope("k", k_in, k_root, kT, g).then_inc(S["qk_ready"], 1)
                after(f"lin_done{q}")
                b, free = next_ab()
                dve.tensor_tensor(grouped(g, vT), by_residue(g, AB[b]), by_residue(g, rstd), ALU.mult) \
                    .then_inc(free, 1)

            def pair(j, last):
                for g in range(GROUPS):
                    if g > 0:
                        qkv(g % 2, g)
                    dilated(g)
                evacuate(y_at[:, j, :], 1)
                after("stats_seen", 240)
                neg, den = (st_x[:, :, :, :, :, w].rearrange("p l g b h -> p l g (b h)") for w in range(2))
                least = cw[:, 1, 0:48].rearrange("p (l b) -> p l b", l=GROUPS)
                e = cw[:, 0, :].rearrange("p (l g b) -> p l g b", l=GROUPS, g=GROUPS)
                ed = cw[:, 2, :].rearrange("p (l g b) -> p l g b", l=GROUPS, g=GROUPS)
                step(dve.tensor_reduce(least, neg.rearrange("p l g b -> p l b g"), AX.X, ALU.min))
                for l in range(GROUPS):
                    op = dve.tensor_tensor(e[:, l], least[:, l].unsqueeze(1).to_broadcast([P, GROUPS, 16]),
                                           neg[:, l], ALU.subtract)
                    if l < GROUPS - 1:
                        step(op)
                op.then_inc(S["shift_ready"], 1)
                after("share_ready")
                for l in range(GROUPS):
                    step(dve.tensor_tensor(ed[:, l], e[:, l], den[:, l], ALU.mult))
                step(dve.tensor_reduce(least, ed.rearrange("p l g b -> p l b g"), AX.X, ALU.add))
                step(dve.reciprocal(least, least))
                for l in range(GROUPS):
                    step(dve.tensor_tensor(least[:, l], least[:, l], e[:, l, l], ALU.mult))
                for l in range(GROUPS):
                    o = O[:, l].rearrange("p b (h d) -> p (b h) d", h=2)
                    op = dve.tensor_tensor(o, o, least[:, l].unsqueeze(2).to_broadcast([P, 16, HD]), ALU.mult)
                    if l < GROUPS - 1:
                        step(op)
                op.then_inc(S["O_scaled"], 1)
                if not last:
                    qkv(0, 0)
                after("combined")
                after("gate_silu")
                b, free = next_cd()
                dve.tensor_tensor(y_at[:, j, :], CD[b][:, :], y_at[:, j, :], ALU.mult).then_inc(free, 1)
                dve.wait_ge(free, n.now(f"cd_free{b}"))

            qkv(0, 0, rotary_tables)
            with n.loop(dve, PAIRS - 1, ab_free0=17, ab_free1=17, cd_free0=20, cd_free1=20, lin_done0=5, lin_done1=5,
                        q_swapped=3, k_swapped=3, q_root_ready=3, k_root_ready=3, dve_step=28, scores_done=24,
                        turned=24, unit_done=24, stats_seen=240, share_ready=1, gate_silu=1, combined=1) as j:
                pair(j, last=False)
            pair(PAIRS - 1, last=True)
            for k in range(PAIRS):
                dve.wait_ge(S["ys_hi"], k + 1)
                dve.tensor_tensor(YS[1][:, k, :], y_at[:, k, :], YS[0][:, k, :].bitcast(F32),
                                  ALU.subtract).then_inc(S["ys_ready"], 1)
            absorb_sum("ple1", HA, halves=True)
            gated_side("mix", HB)

            next_cd()
            after("rstd_ready")
            dve.wait_ge(S["na_mask_loaded"], 16)
            with n.loop(dve, PAIRS // 2, ab_free0=19, ab_free1=19, cd_free0=18, cd_free1=18, lin_done0=3, lin_done1=3,
                        bias_loaded=256, dve_step=6, scores_done=32, turned=32, unit_done=32):
                q = 0
                for _ in range(2):
                    evacuate(nqT[:, :], q)
                    evacuate(nkT[:, :], q ^ 1)
                    after("bias_loaded", 128)
                    for h in range(2):
                        step(dve.scalar_tensor_tensor(bias[h][:, :, :], bias[h][:, :, :], 1.0 / SCALE,
                                                      na_mask[:, :, :], ALU.mult, ALU.add))
                    evacuate(nvT[:, :], q)
                    q ^= 1

                    def bias_of(h, bq):
                        k0, nk, inner = NA_KEYS[bq]
                        r0 = NA_ALL if inner else 2 * (k0 - bq) + 6
                        return bias[h][:, r0:r0 + 2 * nk, :].rearrange("p r c -> p (r c)")

                    attention(lambda bq: NA_KEYS[bq][:2], nsc, bias_of, lambda h, bq: nO[:, bq, h, :],
                              lambda h, bq, w: nst[:, h, w, bq:bq + 1])
                    for b in range(2):
                        dve.wait_ge(S[f"cd_free{b}"], n.now(f"cd_free{b}"))
                    step(dve.reciprocal(nst[:, :, 1, :], nst[:, :, 1, :]))
                    scale = nst[:, :, 1, :].rearrange("p h b -> p b h").unsqueeze(3)
                    dve.tensor_tensor(nO[:, :, :, :], nO[:, :, :, :], scale.to_broadcast([P, BLOCKS, 2, HD]),
                                      ALU.mult).then_inc(S["nO_scaled"], 1)
                    next_cd()

            for b in range(2):
                dve.wait_ge(S[f"cd_free{b}"], n.now(f"cd_free{b}"))
            for name in ("rcos_loaded", "rsin_loaded"):
                dve.wait_ge(S[name], 16)
            dve.wait_ge(S["gamma_ready"], 2)
            with n.loop(dve, RET_HEADS // 2, ab_free0=11, ab_free1=11, cd_free0=5, cd_free1=5, lin_done0=3,
                        lin_done1=3, rq_swapped=1, rk_swapped=1, dve_step=9, diffs_loaded=32, decay_ready=2,
                        rs_done=16, sd_used=16, r_sum=2, r_root_ready=2, gate_silu=2, r_out=2) as i:
                evacuate(rqT[:, :], 0)
                evacuate(rkT[:, :], 1)
                for name, t in (("rq_swapped", rqT), ("rk_swapped", rkT)):
                    after(name)
                    step(dve.tensor_tensor(t[:, :], t[:, :], rcos[:, :], ALU.mult))
                    b, free = next_cd()
                    dve.tensor_tensor(r_m1[:, :], CD[b][:, :], rsin[:, :], ALU.mult).then_inc(free, 1)
                    dve.wait_ge(free, n.now(f"cd_free{b}"))
                    op = dve.tensor_tensor(t[:, :], t[:, :], r_m1[:, :], ALU.add)
                    if t is rqT:
                        step(op)
                op.then_inc(S["rqk_ready"], 1)
                for h in range(2):
                    head = i * 2 + h
                    after("diffs_loaded", 16)
                    step(dve.tensor_scalar(d_neg[:, :], decay_t[:, :], 0.0, lg_col(1, head), ALU.min, ALU.mult))
                    step(dve.tensor_scalar(decay_t[:, :], decay_t[:, :], 0.0, lg_col(0, head), ALU.max, ALU.mult))
                    dve.tensor_tensor(decay_t[:, :], decay_t[:, :], d_neg[:, :], ALU.subtract) \
                        .then_inc(S["decay_arg"], 1)
                    evacuate(rtmp[:, :], 0)
                    evacuate(mix[:, head + PAIRS, :], 1)
                    next_cd()
                    after("decay_ready")
                    for jt in range(BLOCKS):
                        after("rs_done")
                        if jt >= 2:
                            after("sd_used")
                        b, free = next_ab()
                        at = (BLOCKS - 1 - jt) * P
                        dve.tensor_tensor(sd[:, jt % 2, :], AB[b][:, :], decay_t[:, at:at + T],
                                          ALU.mult).then_inc(free, 1)
                    after("sd_used", 2)
                    next_cd()
                    after("r_sum")
                    b, free = next_cd()
                    dve.scalar_tensor_tensor(rtmp[:, :], CD[b][:, :], -1.0 / P, rtmp[:, :], ALU.mult,
                                             ALU.add).then_inc(free, 1)
                    next_cd()
                    after("r_root_ready")
                    step(dve.tensor_tensor(rtmp[:, :], rtmp[:, :], r_root[:, :], ALU.mult))
                    after("gate_silu")
                    gate = mix[:, head + PAIRS, :]
                    dve.scalar_tensor_tensor(gate, rtmp[:, :], dcol("ret_gain", head), gate, ALU.mult,
                                             ALU.mult).then_inc(S["r_out"], 1)
                    dve.wait_ge(S["r_out"], n.next("r_out"))
            for k in range(KT):
                dve.wait_ge(S["mix_hi"], k + 1)
                dve.tensor_tensor(HB[1][:, k, :], mix[:, k, :], HB[0][:, k, :].bitcast(F32),
                                  ALU.subtract).then_inc(S["mix_ready"], 1)
            absorb_sum("mlp", HA)

            next_cd()
            after("rstd_ready")
            with n.loop(dve, FF_CHUNKS, ab_free0=8, ab_free1=8, lin_done0=8, lin_done1=8, u_hi=KT):
                for t in range(KT):
                    after(f"lin_done{t % 2}")
                    b, free = next_ab()
                    dve.scalar_tensor_tensor(ta[:, :], AB[b][:, :], 0.0, rstd[:, :], ALU.max,
                                             ALU.mult).then_inc(free, 1)
                    after("u_hi")
                    dve.tensor_tensor(HB[1][:, t, :], sq[:, :], HB[0][:, t, :].bitcast(F32),
                                      ALU.subtract).then_inc(S["u_ready"], 1)
                for t in range(KT):
                    after(f"lin_done{t % 2}")
                    b, free = next_ab()
                    dve.tensor_tensor(X[:, t, :], X[:, t, :], AB[b][:, :], ALU.add).then_inc(free, 1)
            clear_sum()
            for k in range(KT):
                after("sq_ready")
                dve.tensor_tensor(ssum[:, :], ssum[:, :], sq[:, :], ALU.add).then_inc(S["ssum_added"], 1)
                dve.wait_ge(S["ssum_added"], n.next("ssum_added"))
            next_cd()
            after("rstd_ready")
            for k in range(KT):
                dve.scalar_tensor_tensor(X[:, k, :], X[:, k, :], col("final", k), rstd[:, :], ALU.mult,
                                         ALU.mult).then_inc(S["out_ready"], 1)


def _tables():
    import numpy as np

    f32 = np.float32
    i = np.arange(P)
    own = np.where(i[None, :] <= i[:, None], 0, NEG)
    prev = np.where(i[None, :] >= i[:, None], 0, NEG)
    pair = np.where((i[None, :] <= i[:, None]) & (i[None, :] // HD == i[:, None] // HD), 0, NEG)
    masks = np.concatenate([prev, own, pair], axis=1).astype(f32)
    row, c = i // GRID_W, i % GRID_W
    first = np.clip(c - 8, 0, GRID_W - 16)
    k = np.arange(GRID_W)
    seen = (k[None, :] >= first[:, None]) & (k[None, :] < first[:, None] + 16)
    rows = np.arange(-4, 6)
    near = (rows[None, :] >= row[:, None] - 4) & (rows[None, :] < row[:, None] + 4)
    every = np.broadcast_to(seen[:, None, :], (P, NA_ALL, GRID_W))
    inner = seen[:, None, :] & near[:, :, None]
    na_masks = np.where(np.concatenate([every, inner], axis=1), 0, NEG).astype(f32)
    inv = 1.0 / (f32(10000.0) ** (np.arange(0, HD, 2, dtype=f32) / f32(HD)))
    ang = (inv.astype(f32)[i % HD % (HD // 2)][:, None] * np.arange(T, dtype=f32)[None, :]).astype(f32)
    rot = np.stack([np.cos(ang.astype(np.float64)), np.sin(ang.astype(np.float64))]).astype(f32)

    def swap(half):
        m = np.zeros((P, P), f32)
        for o in range(P):
            d = o % HD
            if d < half:
                m[o + half, o] = -1.0
            elif d < 2 * half:
                m[o - half, o] = 1.0
        return m

    heads = (i[:, None] // HD == i[None, :] // HD).astype(f32)
    mats = np.stack([np.ones((P, P), f32), np.eye(P, dtype=f32), heads, swap(8), swap(HD // 2)])
    span = T + (BLOCKS - 1) * P
    diffs = (np.arange(span)[None, :] - (BLOCKS - 1) * P - i[:, None]).astype(f32)
    rope_inv = 1.0 / (f32(500000.0) ** (np.arange(0, 16, 2, dtype=f32) / f32(16)))
    inv_freq = np.where(i % HD < 16, rope_inv.astype(f32)[i % 8], 0).astype(f32)
    return masks, na_masks, rot, mats, diffs, inv_freq


def _layout(a):
    import numpy as np

    def tiles(m):
        kk, mm = m.shape
        return np.ascontiguousarray(m.reshape(kk // P, P, mm // P, P).transpose(2, 1, 0, 3))

    masks, na_masks, rot, mats, diffs, inv_freq = _tables()
    ci, ai, wi = tiles(a["conv_w_in"][0]), tiles(a["attn_w_in"][0]), tiles(a["w_in_2"][0])
    up, down = tiles(a["w_up_2"][0]), a["w_down_2"][0]
    ple = [tiles(a["ple_w_gate"][i]) for i in range(2)]
    ao = tiles(a["attn_w_out"][0])
    ao = ao.reshape(4, 2, P, 4, P).transpose(0, 2, 1, 3, 4).reshape(4, P, KT, P)
    w = [ci[k * KT + c] for c in range(KT) for k in range(3)]
    w += list(tiles(a["conv_w_out"][0])) + list(ple[0])
    for j in range(PAIRS):
        w += [ai[k * 12 + g * 4 + j] for g in range(GROUPS) for k in range(3)] + [ai[36 + j]]
    w += list(ao) + list(ple[1])
    w += [wi[k * 4 + j] for j in range(PAIRS) for k in range(3)]
    for j in range(2):
        w += [wi[12 + j], wi[14 + j]]
        for h in (2 * j, 2 * j + 1):
            w += [wi[16 + h], wi[20 + h]]
    w += list(tiles(a["w_out_2"][0]))
    for c in range(FF_CHUNKS):
        w += list(up[c * KT:(c + 1) * KT]) + list(tiles(down[c * D:(c + 1) * D]))
    w = np.stack(w).reshape(N_W, P, KT * P)

    def cols(v):
        return v.reshape(-1, P).T

    vecs = np.concatenate(
        [cols(v) for v in (a["norm_g"][0], a["ple_norm_g"][0], a["norm_g"][1], a["ple_norm_g"][1], a["norm_mix_2"][0],
                           a["norm_mlp_2"][0], a["norm_final_2"], a["conv_dw_b"][0], a["conv_ln_g"][0],
                           a["conv_ln_b"][0], a["ret_norm_gain_2"][0], np.tile(a["attn_q_norm"][0], 2),
                           np.tile(a["attn_k_norm"][0], 2), inv_freq)], axis=1)
    decay = np.stack([a["ret_decay_fwd_2"][0], a["ret_decay_bwd_2"][0]])
    out = {
        "x": a["x"][0].T.reshape(KT, P, T),
        "p": a["p"][:, 0].transpose(0, 2, 1).reshape(2, PLE_K, P, T),
        "positions": a["positions"],
        "vecs": vecs,
        "dw": a["conv_dw"][0].reshape(CONV_W, KT, P).transpose(2, 1, 0),
        "w": w,
        "wp": a["ple_w_proj"].reshape(2, PLE_K, P, KT, P).transpose(0, 3, 2, 1, 4),
        "rpb": np.tile(a["na_rpb_2"][0], (1, 1, GRID_W)),
        "decay": np.broadcast_to(decay, (P, 2, RET_HEADS)),
        "masks": masks, "na_masks": na_masks, "rot": rot, "mats": mats, "diffs": diffs,
    }
    return {k: np.ascontiguousarray(v) for k, v in out.items()}


def kernel(**inputs):
    import numpy as np
    from concourse import bacc
    from concourse.bass_utils import run_bass_kernel_spmd

    arrays = _layout({k: np.asarray(v) for k, v in inputs.items()})
    nc = bacc.Bacc("TRN2", target_bir_lowering=False, num_devices=1)
    args = {k: nc.dram_tensor(k + "_dram", v.shape, mybir.dt.from_np(v.dtype), kind="ExternalInput").ap()
            for k, v in arrays.items()}
    args["stats_dram"] = nc.dram_tensor("stats_dram", (GROUPS, T, 4), F32, kind="Internal").ap()
    args["out"] = nc.dram_tensor("out_dram", (KT, P, T), F32, kind="ExternalOutput").ap()
    build(nc, **args)
    r = run_bass_kernel_spmd(nc, [{k + "_dram": v for k, v in arrays.items()}], core_ids=[0])
    return np.ascontiguousarray(r.results[0]["out_dram"].reshape(D, T).T)[None]
```

```python
from collections import defaultdict
from contextlib import ExitStack, contextmanager

import concourse.bass as bass
from concourse import mybir

F32 = mybir.dt.float32
F32R = mybir.dt.float32r
I32 = mybir.dt.int32
ALU = mybir.AluOpType
ACT = mybir.ActivationFunctionType
AX = mybir.AxisListType

P = 128
D = 1024
T = 1024
KT = D // P
HALF = 512
PLE_K = 2
CONV_W = 31
PAD = CONV_W - 1
HD = 64
ROT_HALF = HD // 8
PAIRS = 4
GROUPS = 3
BLOCKS = T // P
GRID_W = 64
NA_ROWS = 8
RET_HEADS = 4
FF_CHUNKS = 4
EPS = 1e-6
NEG = -1e30
SCALE = HD**-0.5
ROUND = 12582912.0
PI = 3.1415925
INV_TWO_PI = 0.15915494309189535
RPB_COLS = 2 * 16 - 1
RPB_ROW = RPB_COLS * GRID_W
RPB_HEAD = (2 * NA_ROWS - 1) * RPB_ROW
TWO_PI_PARTS = (6.28125, 0.0019350051879882812, 3.0199157663446e-07)

POOL_TAPS = 10

NORMS = 7
DVE_OUT = range(5)
POOL_OUT = range(5, KT)

W_TILES = {"conv_in": 24, "conv_out": 8, "ple0": 8, "attn": PAIRS * 10, "attn_out": 4, "ple1": 8,
           "na": PAIRS * 3, "ret": 12, "mix_out": 8, "mlp": 64}
N_W = sum(W_TILES.values())

VEC = {}
_at = 0
for _name, _n in (("norm0", 8), ("ple0", 8), ("norm1", 8), ("ple1", 8), ("mix", 8), ("mlp", 8), ("final", 8),
                  ("dw_b", 8), ("ln_g", 8), ("ln_b", 8), ("ret_gain", 4), ("q_gain", 1), ("k_gain", 1),
                  ("inv_freq", 1)):
    VEC[_name] = _at
    _at += _n
N_VEC = _at

NA_KEYS = [(0, 4, False), (0, 4, False), (0, 5, True), (1, 5, True), (2, 5, True), (3, 5, True),
           (4, 4, False), (4, 4, False)]
NA_ALL = 14
NA_INNER = 10


RAISED = {"ab_free0": "pe", "ab_free1": "pe", "w_ready0": "sp", "w_ready1": "sp", "u_ready": "act",
          "y_ready": "pool"}


class Tally:

    def __init__(self):
        self.base = defaultdict(int, {name: 1 for name in RAISED})
        self.loops = []
        self.cd = 0
        self.ab = 0

    def now(self, name, back=0):
        at = self.base[name] - back
        for i, per in self.loops:
            at = i * per.get(name, 0) + at
        return at

    def next(self, name, n=1):
        self.base[name] += n
        return self.now(name)

    @contextmanager
    def loop(self, eng, count, **per):
        start = dict(self.base)
        with eng.Fori(0, count) as i:
            self.loops.append((i, per))
            yield i
            self.loops.pop()
        found = {k: v - start.get(k, 0) for k, v in self.base.items() if v != start.get(k, 0)}
        assert found == per, f"one pass raises {found}"
        for k, v in per.items():
            self.base[k] = start.get(k, 0) + count * v


class Region:

    def __init__(self, nc, *spans):
        self.nc, self.spans = nc, [list(s) for s in spans]

    def take(self, name, shape, dt=F32):
        n = 4
        for x in shape[1:]:
            n *= x
        for span in self.spans:
            if span[1] - span[0] >= n:
                at = span[0]
                span[0] += -(-n // 32) * 32
                self.at = at
                return self.nc.alloc_sbuf_tensor_at(name, shape, dt, offset=at)
        raise ValueError(f"no room for {name}")


def build(nc, x, p, positions, vecs, dw, w, wp, rpb, decay, masks, na_masks, rot, mats, diffs, stats_dram, out):
    with ExitStack() as ctx:
        class Semaphores(dict):
            def __missing__(self, name):
                self[name] = ctx.enter_context(nc.semaphore(name))
                return self[name]

        S = Semaphores()

        base = -(-nc.sbuf_base // 64) * 64
        end = nc.sbuf_usable_end
        KB = 1024
        X0, HA0, HB0, W0, M0 = base, base + 32 * KB, base + 96 * KB, base + 160 * KB, base + 184 * KB
        X = Region(nc, (X0, HA0)).take("X", [P, KT, T])

        def split_pair(name, at, tiles):
            r = Region(nc, (at, at + 2 * tiles * 4 * KB))
            return r.take(name + "_hi", [P, tiles, T], F32R), r.take(name + "_lo", [P, tiles, T], F32R)

        HA = split_pair("HA", HA0, KT)
        HB = split_pair("HB", HB0, KT)
        rw = Region(nc, (W0, M0))
        w_raw = [rw.take(f"w_raw{i}", [P, KT, P]) for i in range(2)]
        w_hi = [rw.take(f"w_hi{i}", [P, KT, P], F32R) for i in range(2)]
        w_lo = [rw.take(f"w_lo{i}", [P, KT, P], F32R) for i in range(2)]
        rm = Region(nc, (M0, end))
        rstd = rm.take("rstd", [P, T])
        vec = rm.take("vec", [P, N_VEC])
        ones = rm.take("ones", [P, P])
        ident = rm.take("ident", [P, P])
        head_ones = rm.take("head_ones", [P, P])
        perm = rm.take("perm", [P, P])
        eps = rm.take("eps", [P, 1])
        free0 = rm.spans[0][0]
        rt = Region(nc, (free0, end))
        ssum = rt.take("ssum", [P, T])
        sq = rt.take("sq", [P, T])
        ta = rt.take("ta", [P, T])
        wp_sb = [rt.take(f"wp_sb{i}", [P, PLE_K, P]) for i in range(2)]

        def col(name, k=0, n=1):
            return vec[:, VEC[name] + k:VEC[name] + k + n]

        def dcol(name, k):
            return vec[:, bass.ds(k + VEC[name], 1)]

        rc = Region(nc, (X0, HA0))
        ypad = [rc.take(f"ypad{i}", [P, PAD + T]) for i in range(2)]
        sig = rc.take("sig", [P, T])
        acc1 = rc.take("acc1", [P, T])
        accp = [rc.take("accp", [P, T]), ta]
        dw_sb = rc.take("dw_sb", [P, KT, CONV_W])
        act_dw = rc.take("act_dw", [P, CONV_W])
        tap_out = [rc.take(f"tap_out{i}", [P, T]) for i in range(2)]

        def dw_col(c, j):
            return dw_sb[:, bass.ds(c, 1), j:j + 1].rearrange("p a b -> p (a b)")

        ry = Region(nc, (HB0, W0))
        Y = ry.take("Y", [P, KT, T])
        G = ry.take("G", [P, KT, T])

        def side(tag, at):
            a = Region(nc, (at + 28 * KB, at + 32 * KB)).take(f"p_{tag}0", [P, T])
            b = Region(nc, (at + 60 * KB, at + 64 * KB)).take(f"p_{tag}1", [P, T])
            return a, b

        ra = Region(nc, (HB0, W0), (free0, end))
        y_at = ra.take("y_at", [P, PAIRS, T])
        qT, kT, vT, q_in, k_in, cosT, sinT = (
            ra.take(n, [P, T]) for n in ("qT", "kT", "vT", "q_in", "k_in", "cosT", "sinT"))
        V = ra.take("V", [P, BLOCKS, P])
        O = ra.take("O", [P, GROUPS, BLOCKS, P])
        in_o = Region(nc, (ra.at, ra.at + 12 * KB))
        turn_of, turns = in_o.take("turn_of", [P, T]), in_o.take("turns", [P, T])
        pos_i = in_o.take("pos_i", [P, T], I32)
        tmp = ra.take("tmp", [P, T])
        mask = ra.take("mask", [P, 3 * P])
        st = ra.take("st", [P, GROUPS, BLOCKS, 2, 2])
        st_x = ra.take("st_x", [P, GROUPS, GROUPS, BLOCKS, 2, 2])
        cw = ra.take("cw", [P, 3, GROUPS * GROUPS * BLOCKS * 2])
        q_root = ra.take("q_root", [P, T])
        at_q = Region(nc, (ra.at, ra.at + 4 * KB))
        sc = [at_q.take(f"sc{i}", [P, 2, 2 * P]) for i in range(2)]
        k_root = ra.take("k_root", [P, T])
        at_k = Region(nc, (ra.at, ra.at + 4 * KB))
        pt = [at_k.take(f"pt{i}", [P, 4 * P]) for i in range(2)]
        YS = split_pair("YS", HB0 + 32 * KB, PAIRS)

        rmix = Region(nc, (HA0, HB0), (free0, end))
        mix = rmix.take("mix", [P, KT, T])
        nqT, nkT, nvT = (rmix.take(n, [P, T]) for n in ("nqT", "nkT", "nvT"))
        nV = rmix.take("nV", [P, BLOCKS, P])
        na_mask = rmix.take("na_mask", [P, NA_ALL + NA_INNER, GRID_W])
        bias = [rmix.take(f"bias{h}", [P, NA_ALL + NA_INNER, GRID_W]) for h in range(2)]
        nO = rmix.take("nO", [P, BLOCKS, 2, HD])
        NK = 5 * P
        nsc = [rmix.take(f"nsc{i}", [P, NK]) for i in range(2)]
        npt = [rmix.take(f"npt{i}", [P, NK]) for i in range(2)]
        nst = rmix.take("nst", [P, 2, 2, BLOCKS])
        rqT = nqT
        rr = Region(nc, (HA0 + 36 * KB, HB0), (free0, end))
        rkT, rtmp, rcos, rsin = (rr.take(n, [P, T]) for n in ("rkT", "rtmp", "rcos", "rsin"))
        rV = rr.take("rV", [P, BLOCKS, P])
        SPAN = T + (BLOCKS - 1) * P
        decay_t = rr.take("decay_t", [P, SPAN])
        sd = rr.take("sd", [P, 2, T])
        d_neg = Region(nc, (rr.at, rr.at + 8 * KB)).take("d_neg", [P, SPAN])
        lg = rr.take("lg", [P, 2, RET_HEADS])
        r_root, r_m1 = (rr.take(n, [P, T]) for n in ("r_root", "r_m1"))

        def lg_col(way, head):
            return lg[:, way, bass.ds(head, 1)]

        p_a, p_b = side("A", HA0), side("B", HB0)

        AB = [ctx.enter_context(nc.psum_tensor(f"ps_{n}", [P, T], F32)) for n in "AB"]
        CD = [ctx.enter_context(nc.psum_tensor(f"ps_{n}", [P, T], F32)) for n in "CD"]
        OC = T - HD

        block = ctx.enter_context(nc.Block())

        UNITS = [(h, b) for h in range(2) for b in range(BLOCKS)]

        def attn_keys(g, b):
            own = (b, 1, P if g < 2 else 2 * P)
            if (g == 0 and b > 0) or (g == 1 and b % 2):
                return b - 1, 2, 0
            return own

        RES = (1, 4, 16)

        def by_residue(g, t):
            return t[:, :] if g == 0 else t[:, :].rearrange("p (t r) -> p r t", r=RES[g])

        def grouped(g, t):
            return t[:, :] if g == 0 else t[:, :].rearrange("p (r t) -> p r t", r=RES[g])

        def stats_moves(tile, own, g):
            tile = tile.rearrange("p b h s -> p b (h s)")
            d = stats_dram[g]
            if own == 0:
                return [(tile, d.rearrange("(b p) s -> p b s", p=P))]
            if own == 1:
                return [(tile[:, c::2, :], d[c * HALF:(c + 1) * HALF].rearrange("(p r) s -> p r s", r=4))
                        for c in range(2)]
            d = d.rearrange("(i b r) s -> r i b s", b=BLOCKS, r=2)
            return [(tile[c * HD:(c + 1) * HD], d[c]) for c in range(2)]

        @block.sync
        def _(sp):
            n = Tally()
            def weight_pair(t):
                for q in range(2):
                    sp.wait_ge(S[f"w_ready{q}"], n.now(f"w_ready{q}"))
                    n.next(f"w_ready{q}")
                    sp.dma_start(w_raw[q][:, :, :], w[t + q]).then_inc(S[f"w_loaded{q}"], 16)

            for q in range(2):
                sp.sem_inc(S[f"w_ready{q}"], 1)
            sp.dma_start(vec[:, :], vecs).then_inc(S["vec_loaded"], 16)
            sp.dma_start(ones[:, :], mats[0]).then_inc(S["ones_loaded"], 16)
            for k in range(KT):
                if k == 1:
                    weight_pair(0)
                sp.dma_start(X[:, k, :], x[k]).then_inc(S[f"x_loaded{k}"], 16)
            sp.dma_start(ident[:, :], mats[1]).then_inc(S["ident_loaded"], 16)
            sp.dma_start(head_ones[:, :], mats[2]).then_inc(S["head_ones_loaded"], 16)
            sp.dma_start(perm[:, :], mats[3]).then_inc(S["perm_loaded"], 16)

            with n.loop(sp, N_W // 2 - 1, w_ready0=1, w_ready1=1) as i:
                weight_pair(i * 2 + 2)
            for name, ks in (("out_ready", DVE_OUT), ("pool_out_ready", POOL_OUT)):
                for i, k in enumerate(ks):
                    sp.wait_ge(S[name], i + 1)
                    sp.dma_start(out[k], X[:, k, :]).then_inc(S["stored"], 16)
            sp.wait_ge(S["stored"], 16 * KT)

        @block.gpsimd
        def _(pool):
            n = Tally()

            def settle():
                pool.sem_inc(S["pool_settled"], 1)

            def split_lo(q):
                pool.wait_ge(S["w_rounded"], n.next("w_rounded"))
                pool.tensor_tensor(w_lo[q][:, :, :], w_raw[q][:, :, :], w_hi[q][:, :, :].bitcast(F32),
                                   ALU.subtract).then_inc(S[f"w_ready{q}"], 1)

            def split_weights(q):
                pool.wait_ge(S[f"w_loaded{q}"], n.next(f"w_loaded{q}", 16))
                pool.wait_ge(S[f"lin_done{q}"], n.next(f"lin_done{q}"))
                settle()
                pool.tensor_copy(w_hi[q][:, :, :], w_raw[q][:, :, :]).then_inc(S["w_rounded"], 1)
                split_lo(q)

            ADDS = POOL_TAPS - 1
            ADD_ENDS = (0, ADDS // 3, 2 * ADDS // 3, ADDS)

            def add_taps(u, part, first=False):
                for j in range(ADD_ENDS[part], ADD_ENDS[part + 1]):
                    if j == 0:
                        pool.wait_ge(S["tap_product"], n.next("tap_product"))
                        if not first:
                            pool.wait_ge(S["y_ready"], n.now("y_ready"))
                            n.next("y_ready")
                    pool.wait_ge(S["tap_product"], n.next("tap_product"))
                    if j > 0:
                        pool.wait_ge(S["pool_tap"], n.now("pool_tap"))
                    pool.tensor_tensor(accp[u][:, :], (tap_out[0] if j == 0 else accp[u])[:, :],
                                       tap_out[(j + 1) % 2][:, :], ALU.add).then_inc(S["pool_tap"], 1)
                    n.next("pool_tap")

            def conv_pass(u, first):
                for part in range(3):
                    split_lo((u + 1 + part) % 2)
                    add_taps(u ^ 1, part, first)

            pool.sem_inc(S["y_ready"], 1)
            for _ in range(2):
                split_lo(0)
                split_lo(1)
            conv_pass(1, True)
            with n.loop(pool, KT // 2 - 1, w_rounded=6, tap_product=2 * POOL_TAPS, y_ready=2, pool_tap=2 * ADDS):
                conv_pass(0, False)
                conv_pass(1, False)
            split_lo(1)
            for part in range(3):
                add_taps((KT - 1) % 2, part)
            for k in range(KT):
                pool.wait_ge(S["z_hi"], k + 1)
                pool.tensor_tensor(HA[1][:, k, :], Y[:, k, :], HA[0][:, k, :].bitcast(F32),
                                   ALU.subtract).then_inc(S["z_ready"], 1)
            for q in range(2):
                n.next(f"w_loaded{q}", 16 * (W_TILES["conv_in"] // 2 + 1))
                n.next(f"lin_done{q}", W_TILES["conv_in"] // 2)
            with n.loop(pool, (N_W - W_TILES["conv_in"]) // 2 - 1, w_loaded0=16, w_loaded1=16, lin_done0=1,
                        lin_done1=1, w_rounded=2):
                split_weights(0)
                split_weights(1)
            pool.wait_ge(S["rstd_ready"], NORMS)
            for i, k in enumerate(POOL_OUT):
                pool.wait_ge(S["out_gained"], i + 1)
                pool.tensor_tensor(X[:, k, :], X[:, k, :], rstd[:, :], ALU.mult).then_inc(S["pool_out_ready"], 1)

        @block.tensor
        def _(pe):
            n = Tally()

            def take_ab():
                b = n.ab
                n.ab ^= 1
                pe.wait_ge(S[f"ab_free{b}"], n.now(f"ab_free{b}"))
                n.next(f"ab_free{b}")
                return b

            def take_cd():
                b = n.cd
                n.cd ^= 1
                pe.wait_ge(S[f"cd_free{b}"], n.now(f"cd_free{b}"))
                n.next(f"cd_free{b}")
                return b

            def products(b, q, h, ks, w0=0, first=True, last=True):
                hi, lo = h
                for k in ks:
                    for step, (wt, act) in enumerate(((w_hi[q], hi), (w_hi[q], lo), (w_lo[q], hi))):
                        for c in range(2):
                            cols = slice(c * HALF, (c + 1) * HALF)
                            op = pe.matmul(AB[b][:, cols], wt[:, w0 + k, :], act[:, k, cols],
                                           start=(first and k == ks[0] and step == 0),
                                           stop=(last and k == ks[-1] and step == 2))
                return op

            def linear(q, h, pre=None):
                pe.wait_ge(S[f"w_ready{q}"], n.next(f"w_ready{q}"))
                b = take_ab()
                for k in range(KT):
                    if pre:
                        pre(k)
                    op = products(b, q, h, [k], first=(k == 0), last=(k == KT - 1))
                op.then_inc(S[f"lin_done{q}"], 1)
                return b

            def column_sums(src, m, b, first=True, last=True):
                for c in range(2):
                    cols = slice(c * HALF, (c + 1) * HALF)
                    op = pe.matmul(CD[b][:, cols], m[:, :], src[:, cols], start=first, stop=last)
                return op

            def norm_stats():
                pe.wait_ge(S["ssum_added"], n.next("ssum_added", KT))
                column_sums(ssum, ones, take_cd()).then_inc(S["stats_done"], 1)

            def opening(q, h):
                split = n.base["h_ready"]
                linear(q, h, pre=lambda k: pe.wait_ge(S["h_ready"], split + k + 1))
                n.next("h_ready", KT)
                norm_stats()

            for b in range(2):
                pe.sem_inc(S[f"ab_free{b}"], 1)
            pe.wait_ge(S["ones_loaded"], 16)
            opening(0, HA)
            for t in range(1, 5):
                linear(t % 2, HA)
            with n.loop(pe, KT // 2 - 1, w_ready0=3, w_ready1=3, ab_free0=3, ab_free1=3):
                for t in range(6):
                    linear((t + 1) % 2, HA)
            linear(1, HA)
            b = take_cd()
            for k in range(KT):
                pe.wait_ge(S["y_ready"], k + 2)
                op = column_sums(Y[:, k, :], ones, b, k == 0, k == KT - 1)
            op.then_inc(S["y_sum_done"], 1)
            b = take_cd()
            for k in range(KT):
                pe.wait_ge(S["y_sq_ready"], k + 1)
                column_sums((sq, ta)[k % 2], ones, b, k == 0, k == KT - 1).then_inc(S["y_sq_used"], 1)

            def z_ready(k):
                pe.wait_ge(S["z_ready"], k + 1)

            linear(0, HA, pre=z_ready)
            linear(1, HA)
            with n.loop(pe, KT // 2 - 1, w_ready0=1, w_ready1=1, ab_free0=1, ab_free1=1):
                for t in range(2):
                    linear(t, HA)

            def gated_side(h, p_sb):
                def side_tile(t):
                    pe.wait_ge(S[f"wp_loaded{t}"], n.next(f"wp_loaded{t}", 16))
                    b = take_ab()
                    for k in range(PLE_K):
                        for c in range(2):
                            cols = slice(c * HALF, (c + 1) * HALF)
                            op = pe.matmul(AB[b][:, cols], wp_sb[t][:, k, :], p_sb[k][:, cols],
                                           start=(k == 0), stop=(k == PLE_K - 1))
                    op.then_inc(S["side_done"], 1)

                opening(0, h)
                for q in range(2):
                    pe.wait_ge(S[f"p_loaded{q}"], n.next(f"p_loaded{q}", 16))
                side_tile(0)
                linear(1, h)
                side_tile(1)
                with n.loop(pe, KT // 2 - 1, w_ready0=1, w_ready1=1, ab_free0=2, ab_free1=2, wp_loaded0=16,
                            wp_loaded1=16):
                    for t in range(2):
                        linear(t, h)
                        side_tile(t)

            gated_side(HB, p_a)

            def turn(src, count):
                b = take_cd()
                for c in range(count):
                    op = pe.transpose(CD[b][:, c * P:(c + 1) * P], src(c), ident[:, :])
                return b, op

            def neighbourhood(q):
                slots = {}
                pe.wait_ge(S[f"w_ready{q}"], n.next(f"w_ready{q}"))
                tile = take_ab()
                other = tile ^ 1
                for u in range(len(UNITS) + 2):
                    if u < len(UNITS):
                        if u % 2 == 0:
                            op = products(tile, q, HB, [u // 2], first=(u == 0), last=(u == 2 * KT - 2))
                            if u == 2 * KT - 2:
                                op.then_inc(S[f"lin_done{q}"], 1)
                        if u == 0:
                            pe.wait_ge(S[f"ab_free{other}"], n.now(f"ab_free{other}"))
                        else:
                            pe.wait_ge(S["scores_out"], n.next("scores_out"))
                        h, bq = UNITS[u]
                        k0, nk, _ = NA_KEYS[bq]
                        rows = slice(HD * h, HD * h + HD)
                        for c in range(0, nk, 4):
                            cn = min(4, nk - c)
                            op = pe.matmul(AB[other][:, c * P:(c + cn) * P], nqT[rows, bq * P:(bq + 1) * P],
                                           nkT[rows, (k0 + c) * P:(k0 + c + cn) * P], start=True, stop=True)
                        op.then_inc(S["scores_done"], 1)
                    if u == 1:
                        turn(lambda c: nvT[:, c * P:(c + 1) * P], BLOCKS)[1].then_inc(S["v_turned"], 1)
                    if 1 <= u <= len(UNITS):
                        pe.wait_ge(S["probs_ready"], n.next("probs_ready"))
                        nk = NA_KEYS[UNITS[u - 1][1]][1]
                        slots[u - 1], op = turn(lambda c: nsc[(u - 1) % 2][:, c * P:(c + 1) * P], nk)
                        op.then_inc(S["turned"], 1)
                    if u >= 2:
                        h, bq = UNITS[u - 2]
                        k0, nk, _ = NA_KEYS[bq]
                        pe.wait_ge(S["turned_copied"], n.next("turned_copied"))
                        for c in range(nk):
                            op = pe.matmul(CD[slots[u - 2]][:, OC:T], npt[u % 2][:, c * P:(c + 1) * P],
                                           nV[:, k0 + c, HD * h:HD * h + HD], start=(c == 0), stop=(c == nk - 1))
                        op.then_inc(S["unit_done"], 1)
                n.next("scores_out")

            def dilated(g, q):
                slots = {}
                pe.wait_ge(S[f"w_ready{q}"], n.next(f"w_ready{q}"))
                tile = take_ab()
                other = tile ^ 1
                for u in range(BLOCKS + 2):
                    if u < BLOCKS:
                        op = products(tile, q, HA, [u], first=(u == 0), last=(u == KT - 1))
                        if u == KT - 1:
                            op.then_inc(S[f"lin_done{q}"], 1)
                        if u == 0:
                            pe.wait_ge(S["qk_ready"], n.next("qk_ready"))
                            pe.wait_ge(S[f"ab_free{other}"], n.now(f"ab_free{other}"))
                        else:
                            pe.wait_ge(S["scores_out"], n.next("scores_out"))
                        k0, nk, _ = attn_keys(g, u)
                        for h in range(2):
                            rows, at = slice(HD * h, HD * h + HD), h * HALF
                            op = pe.matmul(AB[other][:, at:at + nk * P], qT[rows, u * P:(u + 1) * P],
                                           kT[rows, k0 * P:(k0 + nk) * P], start=True, stop=True)
                        op.then_inc(S["scores_done"], 1)
                    if u == 1:
                        turn(lambda c: vT[:, c * P:(c + 1) * P], BLOCKS)[1].then_inc(S["v_turned"], 1)
                    if 1 <= u <= BLOCKS:
                        pe.wait_ge(S["probs_ready"], n.next("probs_ready"))
                        nk, s = attn_keys(g, u - 1)[1], sc[(u - 1) % 2]
                        slots[u - 1], op = turn(lambda c: s[:, c // nk, c % nk * P:(c % nk + 1) * P], 2 * nk)
                        op.then_inc(S["turned"], 1)
                    if u >= 2:
                        k0, nk, _ = attn_keys(g, u - 2)
                        pe.wait_ge(S["turned_copied"], n.next("turned_copied"))
                        for h in range(2):
                            for c in range(nk):
                                at = (h * nk + c) * P
                                op = pe.matmul(CD[slots[u - 2]][:, T - P + HD * h:T - P + HD * h + HD],
                                               pt[u % 2][:, at:at + P], V[:, k0 + c, HD * h:HD * h + HD],
                                               start=(c == 0), stop=(c == nk - 1))
                        op.then_inc(S["unit_done"], 1)
                n.next("scores_out")

            def head_squares(name):
                pe.wait_ge(S[name + "_sq"], n.next(name + "_sq"))
                column_sums(tmp, head_ones, take_cd()).then_inc(S[name + "_sum"], 1)

            def linear_around(q, at, middle):
                pe.wait_ge(S[f"w_ready{q}"], n.next(f"w_ready{q}"))
                b = take_ab()
                products(b, q, HA, range(at), last=False)
                middle()
                products(b, q, HA, range(at, KT), first=False).then_inc(S[f"lin_done{q}"], 1)

            def kv(q):
                linear_around(q ^ 1, KT // 2, lambda: head_squares("q"))
                linear_around(q, 3, lambda: head_squares("k"))

            def combine():
                pe.wait_ge(S["O_scaled"], n.next("O_scaled"))
                b = take_cd()
                for c in range(2):
                    half = CD[b][:, c * HALF:(c + 1) * HALF]
                    todo = [(0, 4 * c + i, half[:, i * P:(i + 1) * P], ident[:, :]) for i in range(4)]
                    todo += [(1, 2 * r + c, half.rearrange("p (t r) -> p r t", r=4)[:, r, :], ident[:, :])
                             for r in range(4)]
                    todo += [(2, r // 2, half.rearrange("p (t r) -> p r t", r=16)[:, r, :],
                              ident[:, (r % 2) * HD + c * 32:(r % 2) * HD + c * 32 + 32]) for r in range(16)]
                    for i, (g, blk, dst, sel) in enumerate(todo):
                        op = pe.matmul(dst, O[:, g, blk, :], sel, start=(i == 0), stop=(i == len(todo) - 1),
                                       skip_group_check=True)
                op.then_inc(S["combined"], 1)

            def pair(last):
                for g in range(GROUPS):
                    dilated(g, (g + 1) % 2)
                    if g < GROUPS - 1:
                        kv((g + 1) % 2)
                if not last:
                    linear(0, HA)
                    kv(0)
                combine()

            for name in ("head_ones_loaded", "perm_loaded", "ident_loaded"):
                pe.wait_ge(S[name], 16)
            opening(0, HA)
            kv(0)
            with n.loop(pe, PAIRS - 1, w_ready0=5, w_ready1=5, ab_free0=5, ab_free1=5, cd_free0=17, cd_free1=17,
                        q_sq=3, k_sq=3, qk_ready=3, probs_ready=24, turned_copied=24,
                        scores_out=24, O_scaled=1):
                pair(last=False)
            pair(last=True)

            def ys_ready(k):
                pe.wait_ge(S["ys_ready"], k + 1)

            def out_half(t, half, pre=None):
                if half == 0:
                    pe.wait_ge(S[f"w_ready{t}"], n.next(f"w_ready{t}"))
                b = take_ab()
                for k in range(PAIRS):
                    if pre:
                        pre(k)
                    op = products(b, t, YS, [k], w0=half * PAIRS, first=(k == 0), last=(k == PAIRS - 1))
                op.then_inc(S["half_done"] if half == 0 else S[f"lin_done{t}"], 1)

            out_half(0, 0, ys_ready)
            out_half(0, 1)
            out_half(1, 0)
            out_half(1, 1)
            for t in range(2):
                out_half(t, 0)
                out_half(t, 1)
            gated_side(HA, p_b)

            opening(0, HB)
            with n.loop(pe, PAIRS // 2, w_ready0=3, w_ready1=3, ab_free0=3, ab_free1=3, cd_free0=18, cd_free1=18,
                        scores_out=32, probs_ready=32, turned_copied=32, nO_scaled=2):
                def turn_out():
                    pe.wait_ge(S["nO_scaled"], n.next("nO_scaled"))
                    turn(lambda c: nO[:, c, :, :].rearrange("p h d -> p (h d)"), BLOCKS)[1] \
                        .then_inc(S["combined"], 1)

                for t in range(2):
                    linear(t ^ 1, HB)
                    if t == 1:
                        turn_out()
                    linear(t, HB)
                    neighbourhood(t ^ 1)
                turn_out()

            for i in range(RET_HEADS // 2):
                def evacuated(b):
                    pe.wait_ge(S[f"ab_free{b}"], n.now(f"ab_free{b}"))

                bk = linear(1, HB)
                evacuated(bk ^ 1)
                column_sums(rqT, perm, take_cd()).then_inc(S["rq_swapped"], 1)
                evacuated(bk)
                column_sums(rkT, perm, take_cd()).then_inc(S["rk_swapped"], 1)
                bv = linear(0, HB)
                linear(1, HB)
                evacuated(bv)
                turned, op = turn(lambda c: rtmp[:, c * P:(c + 1) * P], BLOCKS)
                op.then_inc(S["v_turned"], 1)
                v_copied = n.now(f"cd_free{turned}")
                pe.wait_ge(S["rqk_ready"], n.next("rqk_ready"))
                for h in range(2):
                    rows = slice(HD * h, HD * h + HD)
                    slots = []
                    for jt in range(BLOCKS + 1):
                        if jt < BLOCKS:
                            b = take_ab()
                            slots.append(b)
                            for c in range(2):
                                cols = slice(c * HALF, (c + 1) * HALF)
                                op = pe.matmul(AB[b][:, cols], rkT[rows, jt * P:(jt + 1) * P], rqT[rows, cols],
                                               start=True, stop=True)
                            op.then_inc(S["rs_done"], 1)
                        if jt == 1:
                            pe.wait_ge(S[f"cd_free{turned}"], v_copied)
                            out_b = take_cd()
                        if jt >= 1:
                            evacuated(slots[jt - 1])
                            for c in range(2):
                                cols = slice(c * HALF, (c + 1) * HALF)
                                op = pe.matmul(CD[out_b][:, cols], rV[:, jt - 1, :], sd[:, (jt - 1) % 2, cols],
                                               start=(jt == 1), stop=(jt == BLOCKS))
                            op.then_inc(S["sd_used"], 1)
                    if h == 0 or i == 0:
                        bv = linear(0, HB)
                    pe.wait_ge(S[f"cd_free{out_b}"], n.now(f"cd_free{out_b}"))
                    column_sums(r_m1, ones, take_cd()).then_inc(S["r_sum"], 1)
                    if h == 0:
                        linear(1, HB)
                        evacuated(bv)
                        turned, op = turn(lambda c: rtmp[:, c * P:(c + 1) * P], BLOCKS)
                        op.then_inc(S["v_turned"], 1)
                        v_copied = n.now(f"cd_free{turned}")
                    pe.wait_ge(S["r_sq_ready"], n.next("r_sq_ready"))
                    column_sums(r_root, ones, take_cd()).then_inc(S["r_var"], 1)

            def mix_ready(k):
                pe.wait_ge(S["mix_ready"], k + 1)

            linear(0, HB, pre=mix_ready)
            linear(1, HB)
            with n.loop(pe, KT // 2 - 1, w_ready0=1, w_ready1=1, ab_free0=1, ab_free1=1):
                for t in range(2):
                    linear(t, HB)

            def down():
                def u_ready(k):
                    pe.wait_ge(S["u_ready"], n.next("u_ready"))

                linear(0, HB, pre=u_ready)
                for t in range(1, KT):
                    linear(t % 2, HB)

            opening(0, HA)
            for t in range(1, KT):
                linear(t % 2, HA)
            down()
            with n.loop(pe, FF_CHUNKS - 1, w_ready0=8, w_ready1=8, ab_free0=8, ab_free1=8, u_ready=KT):
                for t in range(KT):
                    linear(t % 2, HA)
                down()
            norm_stats()

        @block.scalar
        def _(act):
            n = Tally()

            def settle():
                if n.loops:
                    act.sem_inc(S["act_settled"], 1)

            def after(name):
                act.wait_ge(S[name], n.next(name))

            def pass_ab(count=1):
                for _ in range(count):
                    n.next(f"ab_free{n.ab}")
                    n.ab ^= 1

            def after_ab():
                b = n.ab
                n.ab ^= 1
                act.wait_ge(S[f"ab_free{b}"], n.next(f"ab_free{b}"))

            def next_cd():
                b = n.cd
                n.cd ^= 1
                n.next(f"cd_free{b}")
                return b, S[f"cd_free{b}"]

            def inverse_root(dst, b, scale, done):
                act.activation(dst, CD[b][:, :], ACT.Ln, scale=scale, bias=eps[:, :]).then_inc(S[f"cd_free{b}"], 1)
                act.wait_ge(S[f"cd_free{b}"], n.now(f"cd_free{b}"))
                act.activation(dst, dst, ACT.Exp, scale=-0.5).then_inc(S[done], 1)

            def norm_stats():
                after("stats_done")
                b, _ = next_cd()
                inverse_root(rstd[:, :], b, 1.0 / D, "rstd_ready")

            def absorb(gain, hi, xs):
                settle()
                act.activation(hi, xs, ACT.Identity, scale=gain).then_inc(S["hi_ready"], 1)
                act.wait_ge(S["ssum_added"], n.now("ssum_added"))
                n.next("ssum_added")
                settle()
                act.activation(sq[:, :], xs, ACT.Square).then_inc(S["sq_ready"], 1)

            def round_weights(q, first=False):
                act.wait_ge(S[f"w_loaded{q}"], n.next(f"w_loaded{q}", 16))
                if not first:
                    act.wait_ge(S[f"lin_done{q}"], n.next(f"lin_done{q}"))
                act.copy(w_hi[q][:, :, :], w_raw[q][:, :, :]).then_inc(S["w_rounded"], 1)

            act.sem_inc(S["u_ready"], 1)
            act.wait_ge(S["vec_loaded"], 16)
            act.wait_ge(S["consts_set"], 1)
            for k in range(KT):
                act.wait_ge(S[f"x_loaded{k}"], 16)
                absorb(col("norm0", k), HA[0][:, k, :], X[:, k, :])
                if k in (1, 3):
                    round_weights(k // 2, first=True)
            act.wait_ge(S["ssum_added"], KT)
            act.dma_start(dw_sb[:, :, :], dw).then_inc(S["dw_loaded"], 16)
            norm_stats()

            TAP_ENDS = (0, POOL_TAPS // 3, 2 * POOL_TAPS // 3, POOL_TAPS)

            def tap_products(u, c, part):
                if part == 0:
                    act.wait_ge(S["glu_ready"], n.next("glu_ready"))
                    act.wait_ge(S["tap_product"], n.now("tap_product"))
                    settle()
                    act.copy(act_dw[:, :], dw_sb[:, bass.ds(c, 1), :].rearrange("p a b -> p (a b)")) \
                        .then_inc(S["act_dw_ready"], 1)
                    act.wait_ge(S["act_dw_ready"], n.next("act_dw_ready"))
                for j in range(TAP_ENDS[part], TAP_ENDS[part + 1]):
                    at = CONV_W - POOL_TAPS + j
                    if j != 1:
                        sums = 0 if j == 0 else max(j - 2, 1)
                        act.wait_ge(S["pool_tap"], n.now("pool_tap") + sums)
                    act.activation(tap_out[j % 2][:, :], ypad[u][:, at:at + T], ACT.Identity,
                                   scale=act_dw[:, at:at + 1]).then_inc(S["tap_product"], 1)
                    n.next("tap_product")
                if part == 2:
                    n.next("pool_tap", POOL_TAPS - 1)

            def sigmoid():
                pass_ab()
                after_ab()
                act.activation(sig[:, :], sig[:, :], ACT.Sigmoid).then_inc(S["sig_ready"], 1)

            def gate(c):
                after_ab()
                settle()
                act.activation(G[:, c, :], G[:, c, :], ACT.Silu).then_inc(S["gate_silu"], 1)

            def conv_pass(c, u):
                round_weights(u ^ 1)
                tap_products(u ^ 1, c - 1, 0)
                round_weights(u)
                tap_products(u ^ 1, c - 1, 1)
                sigmoid()
                round_weights(u ^ 1)
                tap_products(u ^ 1, c - 1, 2)
                gate(c - 1)

            act.wait_ge(S["dw_loaded"], 16)
            round_weights(0)
            round_weights(1)
            sigmoid()
            conv_pass(1, 1)
            with n.loop(act, KT // 2 - 1, ab_free0=3, ab_free1=3, w_loaded0=48, w_loaded1=48, lin_done0=3,
                        lin_done1=3, glu_ready=2, act_dw_ready=2, pool_tap=2 * (POOL_TAPS - 1),
                        tap_product=2 * POOL_TAPS) as i:
                conv_pass(i * 2 + 2, 0)
                conv_pass(i * 2 + 3, 1)
            round_weights(1)
            for part in range(3):
                tap_products((KT - 1) % 2, KT - 1, part)
            gate(KT - 1)
            act.wait_ge(S["y_ready"], KT + 1)
            for k in range(KT):
                act.dma_start(X[:, k, :], x[k]).then_inc(S[f"x_loaded{k}"], 16)
            after("y_sum_done")
            b, free = next_cd()
            act.activation(ssum[:, :], CD[b][:, :], ACT.Identity, scale=1.0 / D).then_inc(free, 1)
            for k in range(KT):
                after("y_centred")
                if k >= 2:
                    act.wait_ge(S["y_sq_used"], k - 1)
                act.activation((sq, ta)[k % 2][:, :], Y[:, k, :], ACT.Square).then_inc(S["y_sq_ready"], 1)
            act.wait_ge(S["y_sq_used"], KT)
            b, _ = next_cd()
            inverse_root(ssum[:, :], b, 1.0 / D, "ln_rstd_ready")
            for k in range(KT + 1):
                if k < KT:
                    after("ln_scaled")
                    act.activation(Y[:, k, :], Y[:, k, :], ACT.Silu, scale=col("ln_g", k),
                                   bias=col("ln_b", k)).then_inc(S["ln_silu"], 1)
                if k >= 1:
                    after("ln_gated")
                    act.copy(HA[0][:, k - 1, :], Y[:, k - 1, :]).then_inc(S["z_hi"], 1)

            def absorb_sum(name, h):
                with n.loop(act, KT // 2, ab_free0=1, ab_free1=1, ssum_added=2) as i:
                    for t in range(2):
                        after_ab()
                        absorb(dcol(name, i * 2 + t), h[0][:, i * 2 + t, :], X[:, i * 2 + t, :])

            absorb_sum("ple0", HB)

            def gated_side(layer, name, h, p_sb):
                for q in range(2):
                    act.dma_start(p_sb[q][:, :], p[layer, q]).then_inc(S[f"p_loaded{q}"], 16)
                for q in range(2):
                    act.dma_start(wp_sb[q][:, :, :], wp[layer, q]).then_inc(S[f"wp_loaded{q}"], 16)
                norm_stats()

                def side_pass(i, last):
                    for t in range(2):
                        m = i * 2 + t
                        after_ab()
                        act.activation(ta[:, :], ta[:, :], ACT.Sigmoid).then_inc(S["side_gate"], 1)
                        pass_ab()
                        after("x_new")
                        absorb(dcol(name, m), h[0][:, m, :], X[:, m, :])
                        if not last:
                            act.dma_start(wp_sb[t][:, :, :], wp[layer, m + 2]).then_inc(S[f"wp_loaded{t}"], 16)

                with n.loop(act, KT // 2 - 1, ab_free0=2, ab_free1=2, x_new=2, ssum_added=2) as i:
                    side_pass(i, False)
                side_pass(KT // 2 - 1, True)

            gated_side(0, "norm1", HA, p_a)

            norm_stats()
            act.dma_start(pos_i[:, :], bass.AP(tensor=positions.tensor, offset=0, ap=[[0, P], [1, T]])) \
                .then_inc(S["pos_loaded"], 16)
            act.dma_start(mask[:, :], masks).then_inc(S["mask_loaded"], 16)

            def attention(keys, s, t, v, stats):
                def probabilities(u):
                    h, bq = UNITS[u]
                    nk = keys(bq)[1]
                    after("scores_out")
                    act.activation(s[u % 2][:, 0:nk * P], s[u % 2][:, 0:nk * P], ACT.Exp, scale=-1.0,
                                   bias=stats(h, bq, 0), accum_out=stats(h, bq, 1)).then_inc(S["probs_ready"], 1)

                probabilities(0)
                probabilities(1)
                after("v_turned")
                b, free = next_cd()
                act.copy(v[:, :, :].rearrange("p b d -> p (b d)"), CD[b][:, :]).then_inc(free, 1)
                for u in range(len(UNITS)):
                    nk = keys(UNITS[u][1])[1]
                    after("turned")
                    b, _ = next_cd()
                    if u >= 2:
                        after("unit_done")
                    act.copy(t[u % 2][:, 0:nk * P], CD[b][:, 0:nk * P]).then_inc(S["turned_copied"], 1)
                    if u + 2 < len(UNITS):
                        probabilities(u + 2)
                after("unit_done")
                after("unit_done")

            def dilated(g):
                def probabilities(u):
                    nk = attn_keys(g, u)[1]
                    after("scores_out")
                    for h in range(2):
                        s = sc[u % 2][:, h, 0:nk * P]
                        op = act.activation(s, s, ACT.Exp, scale=-1.0, bias=st[:, g, u, h, 0:1],
                                            accum_out=st[:, g, u, h, 1:2])
                    op.then_inc(S["probs_ready"], 1)

                probabilities(0)
                probabilities(1)
                after("v_turned")
                b, free = next_cd()
                act.copy(V[:, :, :].rearrange("p b d -> p (b d)"), CD[b][:, :]).then_inc(free, 1)
                for u in range(BLOCKS):
                    nk = attn_keys(g, u)[1]
                    after("turned")
                    b, _ = next_cd()
                    if u >= 2:
                        after("unit_done")
                    act.copy(pt[u % 2][:, 0:2 * nk * P], CD[b][:, 0:2 * nk * P]).then_inc(S["turned_copied"], 1)
                    if u + 2 < BLOCKS:
                        probabilities(u + 2)
                after("unit_done")
                after("unit_done")

            def sines():
                after("angle_ready")
                act.activation(cosT[:, :], turn_of[:, :], ACT.Sin, scale=0.5).then_inc(S["half_sin"], 1)
                act.activation(sinT[:, :], turn_of[:, :], ACT.Sin).then_inc(S["sin_ready"], 1)

            def roots(between=None):
                for name, src, root, dst in (("q", q_in, q_root, qT), ("k", k_in, k_root, kT)):
                    after_ab()
                    act.activation(tmp[:, :], src[:, :], ACT.Square).then_inc(S[name + "_sq"], 1)
                    act.activation(src[:, :], src[:, :], ACT.Identity, scale=col(name + "_gain")) \
                        .then_inc(S[name + "_gained"], 1)
                    after(name + "_gained")
                    for at in (0, HD):
                        for d, e in ((0, ROT_HALF), (ROT_HALF, 0)):
                            act.dma_start(dst[at + d:at + d + ROT_HALF, :], src[at + e:at + e + ROT_HALF, :]) \
                                .then_inc(S[name + "_swapped"], 16)
                    after(name + "_sum")
                    b, _ = next_cd()
                    inverse_root(root[:, :], b, 1.0 / HD, name + "_root_ready")
                    if between and name == "q":
                        between()
                pass_ab()

            def pair(j, last):
                def load_stats(g):
                    act.wait_ge(S["stats_stored"], n.now("stats_stored"))
                    for own in range(GROUPS):
                        for dst, src in stats_moves(st_x[:, own, g], own, g):
                            act.dma_start(dst, src).then_inc(S["stats_seen"], 16)
                            n.next("stats_seen", 16)

                for g in range(GROUPS):
                    if g > 0:
                        roots()
                        load_stats(g - 1)
                    dilated(g)
                    act.wait_ge(S["probs_ready"], n.next("probs_ready", BLOCKS))
                    for src, dst in stats_moves(st[:, g], g, g):
                        act.dma_start(dst, src).then_inc(S["stats_stored"], 16)
                        n.next("stats_stored", 16)
                load_stats(GROUPS - 1)
                after_ab()
                settle()
                act.activation(y_at[:, j, :], y_at[:, j, :], ACT.Silu).then_inc(S["gate_silu"], 1)
                after("shift_ready")
                act.activation(cw[:, 0, :], cw[:, 0, :], ACT.Exp).then_inc(S["share_ready"], 1)
                if not last:
                    roots()
                next_cd()

            roots(sines)
            with n.loop(act, PAIRS - 1, ab_free0=5, ab_free1=5, cd_free0=17, cd_free1=17, q_sum=3, k_sum=3,
                        q_gained=3, k_gained=3, scores_out=24,
                        v_turned=3, turned=24, unit_done=24, probs_ready=24, stats_stored=80, stats_seen=240,
                        shift_ready=1) as j:
                pair(j, last=False)
            pair(PAIRS - 1, last=True)
            b = n.cd ^ 1
            act.wait_ge(S[f"cd_free{b}"], n.now(f"cd_free{b}"))
            for k in range(PAIRS):
                act.copy(YS[0][:, k, :], y_at[:, k, :]).then_inc(S["ys_hi"], 1)
            absorb_sum("ple1", HA)
            gated_side(1, "mix", HB, p_b)

            norm_stats()
            act.dma_start(na_mask[:, :, :], na_masks).then_inc(S["na_mask_loaded"], 16)

            def load_bias(pair):
                for h in range(2):
                    for d0, count, at in ((1, NA_ALL, 0), (3, NA_INNER, NA_ALL)):
                        for par in (1, 0):
                            row = (pair * 2 + h) * RPB_HEAD + ((d0 - par) * RPB_ROW + RPB_COLS // 2)
                            src = bass.AP(tensor=rpb.tensor, offset=row,
                                          ap=[[RPB_COLS - 1, GRID_W], [RPB_ROW, count], [1, GRID_W]])
                            act.dma_start(bias[h][par * GRID_W:(par + 1) * GRID_W, at:at + count, :], src) \
                                .then_inc(S["bias_loaded"], 16)

            n.next("combined", PAIRS)
            pass_ab()
            with n.loop(act, PAIRS // 2, ab_free0=3, ab_free1=3, cd_free0=18, cd_free1=18, scores_out=32, v_turned=2,
                        turned=32, unit_done=32, combined=2) as i:
                for t in range(2):
                    pair = i * 2 + t
                    if t == 0:
                        load_bias(pair)
                    pass_ab(3)
                    attention(lambda bq: NA_KEYS[bq][:2], nsc, npt, nV,
                              lambda h, bq, w: nst[:, h, w, bq:bq + 1])
                    if t == 0:
                        load_bias(pair + 1)
                    after("combined")
                    b, free = next_cd()
                    settle()
                    act.copy(mix[:, pair, :], CD[b][:, :]).then_inc(free, 1)

            act.wait_ge(free, n.now(f"cd_free{b}"))
            act.dma_start(rcos[:, :], rot[0]).then_inc(S["rcos_loaded"], 16)
            act.dma_start(rsin[:, :], rot[1]).then_inc(S["rsin_loaded"], 16)
            act.dma_start(lg[:, :, :], decay).then_inc(S["decay_loaded"], 16)
            act.wait_ge(S["decay_loaded"], 16)
            act.activation(lg[:, :, :], lg[:, :, :], ACT.Exp).then_inc(S["gamma_ready"], 1)
            act.wait_ge(S["gamma_ready"], 1)
            act.activation(lg[:, :, :], lg[:, :, :], ACT.Ln, scale=-1.0, bias=1.0).then_inc(S["gamma_ready"], 1)
            act.wait_ge(S["gamma_ready"], 2)

            def round_mix(ks):
                for k in ks:
                    act.copy(HB[0][:, k, :], mix[:, k, :]).then_inc(S["mix_hi"], 1)

            for i in range(RET_HEADS // 2):
                def load_diffs():
                    act.dma_start(decay_t[:, :], diffs).then_inc(S["diffs_loaded"], 16)

                def gate(h):
                    pass_ab()
                    after_ab()
                    g = mix[:, i * 2 + h + PAIRS, :]
                    settle()
                    act.activation(g, g, ACT.Silu).then_inc(S["gate_silu"], 1)

                def decay_table():
                    after("decay_arg")
                    act.activation(decay_t[:, :], decay_t[:, :], ACT.Exp).then_inc(S["decay_ready"], 1)

                def values_turned():
                    after("v_turned")
                    b, free = next_cd()
                    act.copy(rV[:, :, :].rearrange("p b d -> p (b d)"), CD[b][:, :]).then_inc(free, 1)

                def head_out():
                    pass_ab(BLOCKS)
                    act.wait_ge(S["sd_used"], n.next("sd_used", BLOCKS))
                    b, free = next_cd()
                    act.activation(r_m1[:, :], CD[b][:, :], ACT.Identity, scale=SCALE).then_inc(free, 1)

                def squares():
                    b, free = next_cd()
                    act.wait_ge(free, n.now(f"cd_free{b}"))
                    act.activation(r_root[:, :], r_m1[:, :], ACT.Square).then_inc(S["r_sq_ready"], 1)

                def head_root():
                    after("r_var")
                    b, _ = next_cd()
                    inverse_root(r_root[:, :], b, 1.0 / P, "r_root_ready")

                pass_ab(1 if i == 0 else 2)
                next_cd()
                next_cd()
                load_diffs()
                gate(0)
                decay_table()
                values_turned()
                head_out()
                load_diffs()
                decay_table()
                squares()
                gate(1)
                values_turned()
                head_root()
                head_out()
                last = i == RET_HEADS // 2 - 1
                if last:
                    round_mix(range(0, 2))
                squares()
                if last:
                    round_mix(range(2, PAIRS))
                head_root()
            for k in range(PAIRS, KT):
                act.wait_ge(S["r_out"], k - PAIRS + 1)
                round_mix([k])
            absorb_sum("mlp", HA)

            norm_stats()
            def up():
                for t in range(KT):
                    after_ab()
                    act.wait_ge(S["u_ready"], n.now("u_ready"))
                    n.next("u_ready")
                    act.activation(sq[:, :], ta[:, :], ACT.Square).then_inc(S["u_sq"], 1)
                    act.wait_ge(S["u_sq"], n.next("u_sq"))
                    act.copy(HB[0][:, t, :], sq[:, :]).then_inc(S["u_hi"], 1)

            with n.loop(act, FF_CHUNKS - 1, ab_free0=8, ab_free1=8, u_sq=KT, u_ready=KT):
                up()
                pass_ab(KT)
            up()
            act.wait_ge(S["u_ready"], n.now("u_ready"))
            for k in range(KT):
                after_ab()
                if k >= 2:
                    after("ssum_added")
                act.activation((sq, ta)[k % 2][:, :], X[:, k, :], ACT.Square).then_inc(S["sq_ready"], 1)
            n.next("ssum_added", 2)
            for k in POOL_OUT:
                act.activation(X[:, k, :], X[:, k, :], ACT.Identity, scale=col("final", k)) \
                    .then_inc(S["out_gained"], 1)
            norm_stats()

        @block.vector
        def _(dve):
            n = Tally()

            def after(name, count=1):
                dve.wait_ge(S[name], n.next(name, count))

            def next_ab():
                b = n.ab
                n.ab ^= 1
                n.next(f"ab_free{b}")
                return b, S[f"ab_free{b}"]

            def next_cd():
                b = n.cd
                n.cd ^= 1
                n.next(f"cd_free{b}")
                return b, S[f"cd_free{b}"]

            def settle():
                if n.loops:
                    dve.sem_inc(S["dve_settled"], 1)

            def step(op):
                op.then_inc(S["dve_step"], 1)
                dve.wait_ge(S["dve_step"], n.next("dve_step"))

            def absorb(gain, h, k, xs):
                after("hi_ready")
                dve.scalar_tensor_tensor(h[1][:, k, :], xs, gain, h[0][:, k, :].bitcast(F32), ALU.mult,
                                         ALU.subtract).then_inc(S["h_ready"], 1)
                after("sq_ready")
                dve.wait_ge(S["ssum_added"], n.now("ssum_added"))
                dve.tensor_tensor(ssum[:, :], ssum[:, :], sq[:, :], ALU.add).then_inc(S["ssum_added"], 1)
                n.next("ssum_added")

            def clear_sum():
                if n.base["ssum_added"]:
                    after("stats_done")
                step(dve.memset(ssum[:, :], 0.0))

            dve.memset(eps[:, :], EPS).then_inc(S["consts_set"], 1)
            dve.wait_ge(S["vec_loaded"], 16)
            clear_sum()
            for k in range(KT):
                dve.wait_ge(S[f"x_loaded{k}"], 16)
                absorb(col("norm0", k), HA, k, X[:, k, :])
            dve.wait_ge(S["h_ready"], KT)
            for u in range(2):
                step(dve.memset(ypad[u][:, 0:PAD], 0.0))
            dve.wait_ge(S["dw_loaded"], 16)
            next_cd()
            after("rstd_ready")

            def evacuate(dst, q, ps=None):
                after(f"lin_done{q}")
                b, free = next_ab()
                dve.tensor_tensor(dst, AB[b][:, :] if ps is None else ps(AB[b]),
                                  rstd[:, :] if ps is None else ps(rstd), ALU.mult).then_inc(free, 1)
                return b

            TAPS = CONV_W - POOL_TAPS
            ENDS = (0, TAPS // 3, 2 * TAPS // 3, TAPS)

            def taps(u, c, part):
                for j in range(ENDS[part], ENDS[part + 1]):
                    tap, win = dw_col(c, j), ypad[u][:, j:j + T]
                    acc = (Y[:, c, :], acc1[:, :])[j % 2]
                    dve.wait_ge(S["dve_tap"], n.now("dve_tap", 1))
                    if j == 0:
                        op = dve.tensor_scalar(acc, win, tap, dcol("dw_b", c), ALU.mult, ALU.add)
                    elif j == 1:
                        op = dve.tensor_scalar(acc, win, tap, None, ALU.mult)
                    else:
                        op = dve.scalar_tensor_tensor(acc, win, tap, acc, ALU.mult, ALU.add)
                    op.then_inc(S["dve_tap"], 1)
                    n.next("dve_tap")
                if part == 2:
                    dve.wait_ge(S["dve_tap"], n.now("dve_tap"))
                    dve.tensor_tensor(Y[:, c, :], Y[:, c, :], acc1[:, :], ALU.add).then_inc(S["dve_tap"], 1)
                    dve.wait_ge(S["dve_tap"], n.next("dve_tap"))

            def add_others(u, c):
                after("pool_tap", POOL_TAPS - 1)
                dve.tensor_tensor(Y[:, c, :], Y[:, c, :], accp[u][:, :], ALU.add).then_inc(S["y_ready"], 1)
                dve.wait_ge(S["y_ready"], n.next("y_ready"))

            def gated_values(u, q, between=lambda: None):
                b = evacuate(ypad[u][:, PAD:], q)
                dve.wait_ge(S[f"ab_free{b}"], n.now(f"ab_free{b}"))
                between()
                evacuate(sig[:, :], q ^ 1)

            def glu(u):
                after("sig_ready")
                dve.tensor_tensor(ypad[u][:, PAD:], ypad[u][:, PAD:], sig[:, :], ALU.mult) \
                    .then_inc(S["glu_ready"], 1)
                dve.wait_ge(S["glu_ready"], n.next("glu_ready"))

            def conv_pass(c, u, first=False):
                taps(u ^ 1, c - 1, 0)
                if not first:
                    after("tap_product", POOL_TAPS)

                def between():
                    if not first:
                        add_others(u, c - 2)
                    taps(u ^ 1, c - 1, 1)

                gated_values(u, u ^ 1, between)
                taps(u ^ 1, c - 1, 2)
                glu(u)
                evacuate(G[:, c - 1, :], u ^ 1)

            dve.memset(acc1[:, 0:1], 0.0).then_inc(S["dve_tap"], 1)
            n.next("dve_tap")
            gated_values(0, 0)
            glu(0)
            conv_pass(1, 1, first=True)
            with n.loop(dve, KT // 2 - 1, ab_free0=3, ab_free1=3, lin_done0=3, lin_done1=3, sig_ready=2, glu_ready=2,
                        dve_tap=2 * (TAPS + 1), pool_tap=2 * (POOL_TAPS - 1), y_ready=2,
                        tap_product=2 * POOL_TAPS) as i:
                conv_pass(i * 2 + 2, 0)
                conv_pass(i * 2 + 3, 1)
            evacuate(G[:, KT - 1, :], 1)
            taps((KT - 1) % 2, KT - 1, 0)
            add_others(KT % 2, KT - 2)
            taps((KT - 1) % 2, KT - 1, 1)
            taps((KT - 1) % 2, KT - 1, 2)
            add_others((KT - 1) % 2, KT - 1)
            b, free = next_cd()
            dve.wait_ge(free, n.now(f"cd_free{b}"))
            for k in range(KT):
                dve.tensor_tensor(Y[:, k, :], Y[:, k, :], ssum[:, :], ALU.subtract).then_inc(S["y_centred"], 1)
            next_cd()
            after("ln_rstd_ready")
            dve.wait_ge(S["gate_silu"], n.next("gate_silu", KT))
            for k in range(KT + 1):
                if k < KT:
                    dve.tensor_tensor(Y[:, k, :], Y[:, k, :], ssum[:, :], ALU.mult).then_inc(S["ln_scaled"], 1)
                if k >= 1:
                    after("ln_silu")
                    dve.tensor_tensor(Y[:, k - 1, :], Y[:, k - 1, :], G[:, k - 1, :], ALU.mult) \
                        .then_inc(S["ln_gated"], 1)
            for k in range(KT):
                dve.wait_ge(S[f"x_loaded{k}"], 32)

            def absorb_sum(name, h, halves=False):
                clear_sum()
                per = dict(half_done=1, lin_done0=1) if halves else dict(lin_done0=1, lin_done1=1)

                def one(m, done):
                    after(done)
                    b, free = next_ab()
                    dve.tensor_tensor(X[:, m, :], X[:, m, :], AB[b][:, :], ALU.add).then_inc(free, 1)
                    dve.wait_ge(free, n.now(f"ab_free{b}"))
                    absorb(dcol(name, m), h, m, X[:, m, :])

                if halves:
                    for m in range(KT):
                        one(m, "half_done" if m % 2 == 0 else f"lin_done{(m // 2) % 2}")
                else:
                    with n.loop(dve, KT // 2, ab_free0=1, ab_free1=1, hi_ready=2, sq_ready=2, ssum_added=2,
                                **per) as i:
                        for t in range(2):
                            one(i * 2 + t, f"lin_done{t}")

            absorb_sum("ple0", HB)

            def gated_side(name, h):
                clear_sum()
                next_cd()
                after("rstd_ready")
                with n.loop(dve, KT // 2, ab_free0=2, ab_free1=2, hi_ready=2, sq_ready=2, ssum_added=2, lin_done0=1,
                            lin_done1=1, side_gate=2, side_done=2, x_new=2) as i:
                    for t in range(2):
                        m = i * 2 + t
                        evacuate(ta[:, :], t)
                        after("side_gate")
                        after("side_done")
                        b, free = next_ab()
                        dve.tensor_tensor(ta[:, :], AB[b][:, :], ta[:, :], ALU.mult).then_inc(free, 1)
                        dve.wait_ge(free, n.now(f"ab_free{b}"))
                        dve.tensor_tensor(X[:, m, :], X[:, m, :], ta[:, :], ALU.add).then_inc(S["x_new"], 1)
                        dve.wait_ge(S["x_new"], n.next("x_new"))
                        absorb(dcol(name, m), h, m, X[:, m, :])

            gated_side("norm1", HA)

            next_cd()
            after("rstd_ready")
            def attention(keys, s, bias_of, out_of, stats):
                other = n.ab ^ 1

                def softmax_input(u):
                    h, bq = UNITS[u]
                    nk = keys(bq)[1]
                    after("scores_done")
                    if u >= 2:
                        after("turned")
                    settle()
                    dve.tensor_tensor_reduce(s[u % 2][:, 0:nk * P], AB[other][:, 0:nk * P], bias_of(h, bq), -SCALE,
                                             3e38, ALU.add, ALU.min, stats(h, bq, 0)).then_inc(S["scores_out"], 1)

                softmax_input(0)
                softmax_input(1)
                next_cd()
                for u in range(len(UNITS)):
                    if u + 2 < len(UNITS):
                        softmax_input(u + 2)
                    after("unit_done")
                    b, free = next_cd()
                    dve.tensor_copy(out_of(*UNITS[u]), CD[b][:, OC:T]).then_inc(free, 1)
                after("turned", 2)

            def dilated(g):
                other = n.ab ^ 1

                def softmax_input(u):
                    _, nk, m = attn_keys(g, u)
                    after("scores_done")
                    if u >= 2:
                        after("turned")
                    settle()
                    for h in range(2):
                        op = dve.tensor_tensor_reduce(sc[u % 2][:, h, 0:nk * P],
                                                      AB[other][:, h * HALF:h * HALF + nk * P],
                                                      mask[:, m:m + nk * P], -SCALE, 3e38, ALU.add, ALU.min,
                                                      st[:, g, u, h, 0:1])
                    op.then_inc(S["scores_out"], 1)

                softmax_input(0)
                softmax_input(1)
                next_cd()
                for u in range(BLOCKS):
                    if u + 2 < BLOCKS:
                        softmax_input(u + 2)
                    after("unit_done")
                    b, free = next_cd()
                    dve.tensor_copy(O[:, g, u, :], CD[b][:, T - P:T]).then_inc(free, 1)
                after("turned", 2)

            def rope(name, src, root, dst, g):
                after(name + "_swapped", 4 * 16)
                dve.tensor_tensor(src[:, :], src[:, :], cosT[:, :], ALU.mult).then_inc(S["dve_step"], 1)
                n.next("dve_step")
                step(dve.tensor_tensor(dst[:, :], dst[:, :], sinT[:, :], ALU.mult))
                step(dve.tensor_tensor(src[:, :], src[:, :], dst[:, :], ALU.add))
                next_cd()
                after(name + "_root_ready")
                return dve.tensor_tensor(grouped(g, dst), by_residue(g, src), by_residue(g, root), ALU.mult)

            def angles():
                dve.wait_ge(S["pos_loaded"], 16)
                step(dve.tensor_copy(turns[:, :], pos_i[:, :]))
                step(dve.tensor_scalar(turn_of[:, :], turns[:, :], col("inv_freq"), None, ALU.mult))
                step(dve.tensor_scalar(turns[:, :], turn_of[:, :], INV_TWO_PI, ROUND, ALU.mult, ALU.add))
                step(dve.tensor_scalar(turns[:, :], turns[:, :], ROUND, None, ALU.subtract))
                for part in TWO_PI_PARTS:
                    step(dve.scalar_tensor_tensor(turn_of[:, :], turns[:, :], -part, turn_of[:, :], ALU.mult, ALU.add))
                dve.tensor_scalar(turn_of[:, :], turn_of[:, :], PI, -PI, ALU.min, ALU.max).then_inc(S["angle_ready"], 1)

            def rotary_tables():
                after("half_sin")
                step(dve.tensor_tensor(cosT[:, :], cosT[:, :], cosT[:, :], ALU.mult))
                step(dve.tensor_scalar(cosT[:, :], cosT[:, :], -2.0, 1.0, ALU.mult, ALU.add))
                after("sin_ready")
                dve.wait_ge(S["mask_loaded"], 16)

            def qkv(q, g, first=False):
                evacuate(q_in[:, :], q)
                if first:
                    angles()
                evacuate(k_in[:, :], q ^ 1)
                if first:
                    rotary_tables()
                step(rope("q", q_in, q_root, qT, g))
                rope("k", k_in, k_root, kT, g).then_inc(S["qk_ready"], 1)
                after(f"lin_done{q}")
                b, free = next_ab()
                dve.tensor_tensor(grouped(g, vT), by_residue(g, AB[b]), by_residue(g, rstd), ALU.mult) \
                    .then_inc(free, 1)

            def pair(j, last):
                for g in range(GROUPS):
                    if g > 0:
                        qkv(g % 2, g)
                    dilated(g)
                evacuate(y_at[:, j, :], 1)
                after("stats_seen", 240)
                neg, den = (st_x[:, :, :, :, :, w].rearrange("p l g b h -> p l g (b h)") for w in range(2))
                least = cw[:, 1, 0:48].rearrange("p (l b) -> p l b", l=GROUPS)
                e = cw[:, 0, :].rearrange("p (l g b) -> p l g b", l=GROUPS, g=GROUPS)
                ed = cw[:, 2, :].rearrange("p (l g b) -> p l g b", l=GROUPS, g=GROUPS)
                step(dve.tensor_reduce(least, neg.rearrange("p l g b -> p l b g"), AX.X, ALU.min))
                for l in range(GROUPS):
                    op = dve.tensor_tensor(e[:, l], least[:, l].unsqueeze(1).to_broadcast([P, GROUPS, 16]),
                                           neg[:, l], ALU.subtract)
                    if l < GROUPS - 1:
                        step(op)
                op.then_inc(S["shift_ready"], 1)
                after("share_ready")
                for l in range(GROUPS):
                    step(dve.tensor_tensor(ed[:, l], e[:, l], den[:, l], ALU.mult))
                step(dve.tensor_reduce(least, ed.rearrange("p l g b -> p l b g"), AX.X, ALU.add))
                step(dve.reciprocal(least, least))
                for l in range(GROUPS):
                    step(dve.tensor_tensor(least[:, l], least[:, l], e[:, l, l], ALU.mult))
                for l in range(GROUPS):
                    o = O[:, l].rearrange("p b (h d) -> p (b h) d", h=2)
                    op = dve.tensor_tensor(o, o, least[:, l].unsqueeze(2).to_broadcast([P, 16, HD]), ALU.mult)
                    if l < GROUPS - 1:
                        step(op)
                op.then_inc(S["O_scaled"], 1)
                if not last:
                    qkv(0, 0)
                after("combined")
                after("gate_silu")
                b, free = next_cd()
                dve.tensor_tensor(y_at[:, j, :], CD[b][:, :], y_at[:, j, :], ALU.mult).then_inc(free, 1)
                dve.wait_ge(free, n.now(f"cd_free{b}"))

            for dst in (qT, kT):
                step(dve.memset(dst[:, :], 0.0))
            qkv(0, 0, first=True)
            with n.loop(dve, PAIRS - 1, ab_free0=5, ab_free1=5, cd_free0=17, cd_free1=17, lin_done0=5, lin_done1=5,
                        q_swapped=192, k_swapped=192, q_root_ready=3, k_root_ready=3, dve_step=34, scores_done=24,
                        turned=24, unit_done=24, stats_seen=240, share_ready=1, gate_silu=1, combined=1) as j:
                pair(j, last=False)
            pair(PAIRS - 1, last=True)
            for k in range(PAIRS):
                dve.wait_ge(S["ys_hi"], k + 1)
                dve.tensor_tensor(YS[1][:, k, :], y_at[:, k, :], YS[0][:, k, :].bitcast(F32),
                                  ALU.subtract).then_inc(S["ys_ready"], 1)
            absorb_sum("ple1", HA, halves=True)
            gated_side("mix", HB)

            next_cd()
            after("rstd_ready")
            dve.wait_ge(S["na_mask_loaded"], 16)
            evacuate(nqT[:, :], 0)
            with n.loop(dve, PAIRS // 2, ab_free0=3, ab_free1=3, cd_free0=18, cd_free1=18, lin_done0=3, lin_done1=3,
                        bias_loaded=256, dve_step=6, scores_done=32, turned=32, unit_done=32):
                for t in range(2):
                    evacuate(nkT[:, :], t ^ 1)
                    after("bias_loaded", 128)
                    for h in range(2):
                        step(dve.scalar_tensor_tensor(bias[h][:, :, :], bias[h][:, :, :], 1.0 / SCALE,
                                                      na_mask[:, :, :], ALU.mult, ALU.add))
                    evacuate(nvT[:, :], t)

                    def bias_of(h, bq):
                        k0, nk, inner = NA_KEYS[bq]
                        r0 = NA_ALL if inner else 2 * (k0 - bq) + 6
                        return bias[h][:, r0:r0 + 2 * nk, :].rearrange("p r c -> p (r c)")

                    attention(lambda bq: NA_KEYS[bq][:2], nsc, bias_of, lambda h, bq: nO[:, bq, h, :],
                              lambda h, bq, w: nst[:, h, w, bq:bq + 1])
                    for b in range(2):
                        dve.wait_ge(S[f"cd_free{b}"], n.now(f"cd_free{b}"))
                    step(dve.reciprocal(nst[:, :, 1, :], nst[:, :, 1, :]))
                    scale = nst[:, :, 1, :].rearrange("p h b -> p b h").unsqueeze(3)
                    dve.tensor_tensor(nO[:, :, :, :], nO[:, :, :, :], scale.to_broadcast([P, BLOCKS, 2, HD]),
                                      ALU.mult).then_inc(S["nO_scaled"], 1)
                    next_cd()
                    evacuate(nqT[:, :], t ^ 1)

            for b in range(2):
                dve.wait_ge(S[f"cd_free{b}"], n.now(f"cd_free{b}"))
            for name in ("rcos_loaded", "rsin_loaded"):
                dve.wait_ge(S[name], 16)
            dve.wait_ge(S["gamma_ready"], 2)

            def mix_rest(ks):
                for k in ks:
                    dve.wait_ge(S["mix_hi"], k + 1)
                    dve.tensor_tensor(HB[1][:, k, :], mix[:, k, :], HB[0][:, k, :].bitcast(F32),
                                      ALU.subtract).then_inc(S["mix_ready"], 1)

            for i in range(RET_HEADS // 2):
                if i:
                    evacuate(rqT[:, :], 0)
                evacuate(rkT[:, :], 1)
                for name, t in (("rq_swapped", rqT), ("rk_swapped", rkT)):
                    after(name)
                    step(dve.tensor_tensor(t[:, :], t[:, :], rcos[:, :], ALU.mult))
                    b, free = next_cd()
                    dve.tensor_tensor(r_m1[:, :], CD[b][:, :], rsin[:, :], ALU.mult).then_inc(free, 1)
                    dve.wait_ge(free, n.now(f"cd_free{b}"))
                    op = dve.tensor_tensor(t[:, :], t[:, :], r_m1[:, :], ALU.add)
                    if t is rqT:
                        step(op)
                op.then_inc(S["rqk_ready"], 1)

                def decay_args(h):
                    head = i * 2 + h
                    after("diffs_loaded", 16)
                    step(dve.tensor_scalar(d_neg[:, :], decay_t[:, :], 0.0, lg_col(1, head), ALU.min, ALU.mult))
                    step(dve.tensor_scalar(decay_t[:, :], decay_t[:, :], 0.0, lg_col(0, head), ALU.max, ALU.mult))
                    dve.tensor_tensor(decay_t[:, :], decay_t[:, :], d_neg[:, :], ALU.subtract) \
                        .then_inc(S["decay_arg"], 1)

                def less_mean():
                    after("r_sum")
                    b, free = next_cd()
                    dve.scalar_tensor_tensor(r_m1[:, :], CD[b][:, :], -1.0 / P, r_m1[:, :], ALU.mult,
                                             ALU.add).then_inc(free, 1)

                def finish(h):
                    after("r_root_ready")
                    step(dve.tensor_tensor(r_m1[:, :], r_m1[:, :], r_root[:, :], ALU.mult))
                    after("gate_silu")
                    gate = mix[:, i * 2 + h + PAIRS, :]
                    dve.scalar_tensor_tensor(gate, r_m1[:, :], dcol("ret_gain", i * 2 + h), gate, ALU.mult,
                                             ALU.mult).then_inc(S["r_out"], 1)
                    dve.wait_ge(S["r_out"], n.next("r_out"))

                def decayed(h):
                    after("decay_ready")
                    for jt in range(BLOCKS):
                        after("rs_done")
                        if jt >= 2:
                            after("sd_used")
                        b, free = next_ab()
                        at = (BLOCKS - 1 - jt) * P
                        dve.tensor_tensor(sd[:, jt % 2, :], AB[b][:, :], decay_t[:, at:at + T],
                                          ALU.mult).then_inc(free, 1)
                        if h == 1 and jt == 3:
                            finish(0)
                    after("sd_used", 2)
                    next_cd()

                decay_args(0)
                evacuate(rtmp[:, :], 0)
                evacuate(mix[:, i * 2 + PAIRS, :], 1)
                next_cd()
                decayed(0)
                decay_args(1)
                evacuate(rtmp[:, :], 0)
                less_mean()
                evacuate(mix[:, i * 2 + 1 + PAIRS, :], 1)
                next_cd()
                next_cd()
                decayed(1)
                less_mean()
                next_cd()
                if i == RET_HEADS // 2 - 1:
                    mix_rest(range(PAIRS))
                finish(1)
            mix_rest(range(PAIRS, KT))
            absorb_sum("mlp", HA)

            next_cd()
            after("rstd_ready")
            def up():
                for t in range(KT):
                    after(f"lin_done{t % 2}")
                    b, free = next_ab()
                    dve.scalar_tensor_tensor(ta[:, :], AB[b][:, :], 0.0, rstd[:, :], ALU.max,
                                             ALU.mult).then_inc(free, 1)
                    after("u_hi")
                    dve.tensor_tensor(HB[1][:, t, :], sq[:, :], HB[0][:, t, :].bitcast(F32),
                                      ALU.subtract).then_inc(S["u_ready"], 1)

            def down(t):
                after(f"lin_done{t % 2}")
                b, free = next_ab()
                dve.tensor_tensor(X[:, t, :], X[:, t, :], AB[b][:, :], ALU.add).then_inc(free, 1)

            with n.loop(dve, FF_CHUNKS - 1, ab_free0=8, ab_free1=8, lin_done0=8, lin_done1=8, u_hi=KT):
                up()
                for t in range(KT):
                    down(t)
            up()
            clear_sum()
            for t in range(KT + 1):
                if t < KT:
                    down(t)
                if t >= 1:
                    after("sq_ready")
                    dve.wait_ge(S["ssum_added"], n.now("ssum_added"))
                    dve.tensor_tensor(ssum[:, :], ssum[:, :], (sq, ta)[(t - 1) % 2][:, :],
                                      ALU.add).then_inc(S["ssum_added"], 1)
                    n.next("ssum_added")
            next_cd()
            after("rstd_ready")
            for k in DVE_OUT:
                dve.scalar_tensor_tensor(X[:, k, :], X[:, k, :], col("final", k), rstd[:, :], ALU.mult,
                                         ALU.mult).then_inc(S["out_ready"], 1)


def _tables():
    import numpy as np

    f32 = np.float32
    i = np.arange(P)
    own = np.where(i[None, :] <= i[:, None], 0, NEG)
    prev = np.where(i[None, :] >= i[:, None], 0, NEG)
    pair = np.where((i[None, :] <= i[:, None]) & (i[None, :] // HD == i[:, None] // HD), 0, NEG)
    masks = np.concatenate([prev, own, pair], axis=1).astype(f32)
    row, c = i // GRID_W, i % GRID_W
    first = np.clip(c - 8, 0, GRID_W - 16)
    k = np.arange(GRID_W)
    seen = (k[None, :] >= first[:, None]) & (k[None, :] < first[:, None] + 16)
    rows = np.arange(-4, 6)
    near = (rows[None, :] >= row[:, None] - 4) & (rows[None, :] < row[:, None] + 4)
    every = np.broadcast_to(seen[:, None, :], (P, NA_ALL, GRID_W))
    inner = seen[:, None, :] & near[:, :, None]
    na_masks = np.where(np.concatenate([every, inner], axis=1), 0, NEG).astype(f32)
    inv = 1.0 / (f32(10000.0) ** (np.arange(0, HD, 2, dtype=f32) / f32(HD)))
    ang = (inv.astype(f32)[i % HD % (HD // 2)][:, None] * np.arange(T, dtype=f32)[None, :]).astype(f32)
    rot = np.stack([np.cos(ang.astype(np.float64)), np.sin(ang.astype(np.float64))]).astype(f32)

    def swap(half):
        m = np.zeros((P, P), f32)
        for o in range(P):
            d = o % HD
            if d < half:
                m[o + half, o] = -1.0
            elif d < 2 * half:
                m[o - half, o] = 1.0
        return m

    heads = (i[:, None] // HD == i[None, :] // HD).astype(f32)
    mats = np.stack([np.ones((P, P), f32), np.eye(P, dtype=f32), heads, swap(HD // 2)])
    span = T + (BLOCKS - 1) * P
    diffs = (np.arange(span)[None, :] - (BLOCKS - 1) * P - i[:, None]).astype(f32)
    rope_inv = 1.0 / (f32(500000.0) ** (np.arange(0, 16, 2, dtype=f32) / f32(16)))
    sign = np.where(i % HD < ROT_HALF, -1, 1)
    inv_freq = np.where(i % HD < 2 * ROT_HALF, sign * rope_inv.astype(f32)[i % ROT_HALF], 0).astype(f32)
    return masks, na_masks, rot, mats, diffs, inv_freq


def _layout(a):
    import numpy as np

    def tiles(m):
        kk, mm = m.shape
        return np.ascontiguousarray(m.reshape(kk // P, P, mm // P, P).transpose(2, 1, 0, 3))

    masks, na_masks, rot, mats, diffs, inv_freq = _tables()
    ci, ai, wi = tiles(a["conv_w_in"][0]), tiles(a["attn_w_in"][0]), tiles(a["w_in_2"][0])
    up, down = tiles(a["w_up_2"][0]), a["w_down_2"][0]
    ple = [tiles(a["ple_w_gate"][i]) for i in range(2)]
    ao = tiles(a["attn_w_out"][0])
    ao = ao.reshape(4, 2, P, 4, P).transpose(0, 2, 1, 3, 4).reshape(4, P, KT, P)
    w = []
    for c in range(KT):
        w += [ci[c], ci[KT + c]] + ([ci[2 * KT + c - 1]] if c else [])
    w += [ci[3 * KT - 1]]
    w += list(tiles(a["conv_w_out"][0])) + list(ple[0])
    for j in range(PAIRS):
        w += [ai[k * 12 + g * 4 + j] for g in range(GROUPS) for k in range(3)] + [ai[36 + j]]
    w += list(ao) + list(ple[1])
    w += [wi[k * 4 + j] for j in range(PAIRS) for k in range(3)]
    for j in range(2):
        w += [wi[12 + j], wi[14 + j]]
        for h in (2 * j, 2 * j + 1):
            w += [wi[16 + h], wi[20 + h]]
    w += list(tiles(a["w_out_2"][0]))
    for c in range(FF_CHUNKS):
        w += list(up[c * KT:(c + 1) * KT]) + list(tiles(down[c * D:(c + 1) * D]))
    w = np.stack(w).reshape(N_W, P, KT * P)

    def cols(v):
        return v.reshape(-1, P).T

    vecs = np.concatenate(
        [cols(v) for v in (a["norm_g"][0], a["ple_norm_g"][0], a["norm_g"][1], a["ple_norm_g"][1], a["norm_mix_2"][0],
                           a["norm_mlp_2"][0], a["norm_final_2"], a["conv_dw_b"][0], a["conv_ln_g"][0],
                           a["conv_ln_b"][0], a["ret_norm_gain_2"][0], np.tile(a["attn_q_norm"][0], 2),
                           np.tile(a["attn_k_norm"][0], 2), inv_freq)], axis=1)
    decay = np.stack([a["ret_decay_fwd_2"][0], a["ret_decay_bwd_2"][0]])
    out = {
        "x": a["x"][0].T.reshape(KT, P, T),
        "p": a["p"][:, 0].transpose(0, 2, 1).reshape(2, PLE_K, P, T),
        "positions": a["positions"],
        "vecs": vecs,
        "dw": a["conv_dw"][0].reshape(CONV_W, KT, P).transpose(2, 1, 0),
        "w": w,
        "wp": a["ple_w_proj"].reshape(2, PLE_K, P, KT, P).transpose(0, 3, 2, 1, 4),
        "rpb": np.tile(a["na_rpb_2"][0], (1, 1, GRID_W)),
        "decay": np.broadcast_to(decay, (P, 2, RET_HEADS)),
        "masks": masks, "na_masks": na_masks, "rot": rot, "mats": mats, "diffs": diffs,
    }
    return {k: np.ascontiguousarray(v) for k, v in out.items()}


def kernel(**inputs):
    import numpy as np
    from concourse import bacc
    from concourse.bass_utils import run_bass_kernel_spmd

    arrays = _layout({k: np.asarray(v) for k, v in inputs.items()})
    nc = bacc.Bacc("TRN2", target_bir_lowering=False, num_devices=1)
    args = {k: nc.dram_tensor(k + "_dram", v.shape, mybir.dt.from_np(v.dtype), kind="ExternalInput").ap()
            for k, v in arrays.items()}
    args["stats_dram"] = nc.dram_tensor("stats_dram", (GROUPS, T, 4), F32, kind="Internal").ap()
    args["out"] = nc.dram_tensor("out_dram", (KT, P, T), F32, kind="ExternalOutput").ap()
    build(nc, **args)
    r = run_bass_kernel_spmd(nc, [{k + "_dram": v for k, v in arrays.items()}], core_ids=[0])
    return np.ascontiguousarray(r.results[0]["out_dram"].reshape(D, T).T)[None]
```
